# Optimizing a Trainium2 kernel written in Bass

```python
import math
import jax, jax.numpy as jnp
from jax import lax
import numpy as np

D_MODEL = 1024
BATCH = 1
SEQ = 256
DEPTH = 2

HEAD_DIM = 64
ROPE_THETA = 10000.0
NORM_EPS = 1e-6
D_FF = 2816
BAND_BLOCK = 128
GATHER_CHUNK = 32
NEG_INF = -1e30
FORCE_SCORE = 1e4

A_Q_HEADS = 8
A_KV_HEADS = 2
A_WINDOW = 128
B_Q_HEADS = 8
B_KV_HEADS = 2
NSA_CMP_LEN = 32
NSA_CMP_STRIDE = 16
NSA_CMP_HIDDEN = 256
NSA_SEL_LEN = 64
NSA_SEL_COUNT = 8
NSA_WINDOW = 512
C_GROUPS = ((128, 1), (512, 4), (2048, 16))
C_HEADS_PER_GROUP = 4
C_HEADS = len(C_GROUPS) * C_HEADS_PER_GROUP
D_HEADS = 4
MOBA_BLOCK = 256
MOBA_TOPK = 3

EVEN_SIZES = ([A_Q_HEADS * HEAD_DIM] + [A_KV_HEADS * HEAD_DIM] * 2 + [B_Q_HEADS * HEAD_DIM]
              + [B_KV_HEADS * HEAD_DIM] * 6 + [3 * B_Q_HEADS])
EVEN_IN = sum(EVEN_SIZES)
EVEN_OUT = (A_Q_HEADS + B_Q_HEADS) * HEAD_DIM
ODD_SIZES = [C_HEADS * HEAD_DIM] * 3 + [D_HEADS * HEAD_DIM] * 3
ODD_IN = sum(ODD_SIZES)
ODD_OUT = (C_HEADS_PER_GROUP + D_HEADS) * HEAD_DIM
N_EVEN = (DEPTH + 1) // 2
N_ODD = DEPTH // 2

kernel_name = "hybrid_swa_nsa_dilated_moba_macaron"

def rms_norm(x, g):
    xf = x.astype(jnp.float32)
    y = xf * lax.rsqrt(jnp.mean(xf * xf, axis=-1, keepdims=True) + NORM_EPS)
    return (y * g.astype(jnp.float32)).astype(x.dtype)

def swiglu(x, wi, wo):
    gate, up = jnp.split(x @ wi, 2, axis=-1)
    return (jax.nn.silu(gate) * up) @ wo

def rope(x):
    T, dh = x.shape[-2], x.shape[-1]
    inv = 1.0 / (ROPE_THETA ** (jnp.arange(0, dh, 2, dtype=jnp.float32) / dh))
    ang = jnp.arange(T, dtype=jnp.float32)[:, None] * inv[None, :]
    cos = jnp.cos(ang).astype(x.dtype)
    sin = jnp.sin(ang).astype(x.dtype)
    x1, x2 = jnp.split(x, 2, axis=-1)
    return jnp.concatenate([x1 * cos - x2 * sin, x2 * cos + x1 * sin], axis=-1)

def to_heads(z, n):
    B, T, _ = z.shape
    return z.reshape(B, T, n, HEAD_DIM).transpose(0, 2, 1, 3)

def from_heads(o):
    B, H, T, dh = o.shape
    return o.transpose(0, 2, 1, 3).reshape(B, T, H * dh)

def split_cols(z, sizes):
    offs = []
    acc = 0
    for s in sizes[:-1]:
        acc += s
        offs.append(acc)
    return jnp.split(z, offs, axis=-1)

def masked_softmax_stats(s, mask, sink=None):
    s = jnp.where(mask, s, NEG_INF)
    m = jnp.max(s, axis=-1)
    if sink is not None:
        m = jnp.maximum(m, sink)
    p = jnp.where(mask, jnp.exp(s - m[..., None]), 0.0)
    denom = jnp.sum(p, axis=-1)
    if sink is not None:
        denom = denom + jnp.exp(sink - m)
    denom = jnp.where(denom > 0, denom, 1.0)
    return p, m, denom

def banded_attention(q, k, v, max_dist, sink=None):
    B, Hk, G, L, dh = q.shape
    bq = math.gcd(L, BAND_BLOCK)
    nb = L // bq
    nw = -(-max_dist // bq)
    pad = nw * bq
    kp = jnp.pad(k, ((0, 0), (0, 0), (pad, 0), (0, 0))).reshape(B, Hk, nb + nw, bq, dh)
    vp = jnp.pad(v, ((0, 0), (0, 0), (pad, 0), (0, 0))).reshape(B, Hk, nb + nw, bq, dh)
    kwin = jnp.concatenate([kp[:, :, j:j + nb] for j in range(nw + 1)], axis=3)
    vwin = jnp.concatenate([vp[:, :, j:j + nb] for j in range(nw + 1)], axis=3)
    qb = q.reshape(B, Hk, G, nb, bq, dh)
    s = jnp.einsum('bhgnqd,bhnkd->bhgnqk', qb, kwin).astype(jnp.float32) * (dh ** -0.5)
    qpos = jnp.arange(nb)[:, None] * bq + jnp.arange(bq)[None, :]
    kpos = jnp.arange(nb)[:, None] * bq - pad + jnp.arange((nw + 1) * bq)[None, :]
    dist = qpos[:, :, None] - kpos[:, None, :]
    mask = (dist >= 0) & (dist <= max_dist) & (kpos[:, None, :] >= 0)
    sink_b = None if sink is None else sink.astype(jnp.float32)[None, :, :, None, None]
    p, m, denom = masked_softmax_stats(s, mask, sink_b)
    o = jnp.einsum('bhgnqk,bhnkd->bhgnqd', p.astype(v.dtype), vwin).astype(jnp.float32)
    o = (o / denom[..., None]).astype(q.dtype)
    lse = m + jnp.log(denom)
    return o.reshape(B, Hk, G, L, dh), lse.reshape(B, Hk, G, L)

def gathered_block_attention(q, k_blocks, v_blocks, idx, valid):
    B, Hk, G, T, dh = q.shape
    bs = k_blocks.shape[3]
    K = idx.shape[-1]
    c = math.gcd(T, GATHER_CHUNK)
    nc = T // c
    qs = jnp.moveaxis(q.reshape(B, Hk, G, nc, c, dh), 3, 0)
    ids = jnp.moveaxis(idx.reshape(B, Hk, nc, c, K), 2, 0)
    vals = jnp.moveaxis(valid.reshape(B, Hk, nc, c, K), 2, 0)
    poss = jnp.arange(T).reshape(nc, c)
    take = jax.vmap(jax.vmap(lambda blocks, ix: blocks[ix]))
    scale = dh ** -0.5

    def chunk(args):
        qc, ic, vc, pc = args
        kg = take(k_blocks, ic).reshape(B, Hk, c, K * bs, dh)
        vg = take(v_blocks, ic).reshape(B, Hk, c, K * bs, dh)
        kpos = (ic[..., None] * bs + jnp.arange(bs)).reshape(B, Hk, c, K * bs)
        mask = jnp.repeat(vc, bs, axis=-1) & (kpos <= pc[:, None])
        s = jnp.einsum('bhgcd,bhckd->bhgck', qc, kg).astype(jnp.float32) * scale
        p, _, denom = masked_softmax_stats(s, mask[:, :, None])
        o = jnp.einsum('bhgck,bhckd->bhgcd', p.astype(vg.dtype), vg).astype(jnp.float32)
        return (o / denom[..., None]).astype(q.dtype)

    out = lax.map(chunk, (qs, ids, vals, poss))
    return jnp.moveaxis(out, 0, 3).reshape(B, Hk, G, T, dh)

def nsa_attention(q, k_cmp, v_cmp, k_sel, v_sel, k_win, v_win, gate_logits, cmp_pe, cmp_w1, cmp_w2):
    B, Hq, T, dh = q.shape
    Hk = k_cmp.shape[1]
    G = Hq // Hk
    scale = dh ** -0.5
    qg = q.reshape(B, Hk, G, T, dh)
    qr = rope(q).reshape(B, Hk, G, T, dh)
    t = jnp.arange(T)
    nc = (T - NSA_CMP_LEN) // NSA_CMP_STRIDE + 1
    starts = jnp.arange(nc) * NSA_CMP_STRIDE
    win = starts[:, None] + jnp.arange(NSA_CMP_LEN)[None, :]

    def compress(z, pe, w1, w2):
        zb = z[:, :, win] + pe
        return jax.nn.gelu(zb.reshape(B, Hk, nc, NSA_CMP_LEN * dh) @ w1) @ w2

    kc = compress(k_cmp, cmp_pe[0], cmp_w1[0], cmp_w2[0])
    vc = compress(v_cmp, cmp_pe[1], cmp_w1[1], cmp_w2[1])
    cmask = (starts + NSA_CMP_LEN - 1)[None, :] <= t[:, None]
    s = jnp.einsum('bhgtd,bhnd->bhgtn', qg, kc).astype(jnp.float32) * scale
    p, _, denom = masked_softmax_stats(s, cmask)
    p_cmp = p / denom[..., None]
    o_cmp = jnp.einsum('bhgtn,bhnd->bhgtd', p_cmp.astype(vc.dtype), vc)
    nsb = T // NSA_SEL_LEN
    sel_start = jnp.arange(nsb) * NSA_SEL_LEN
    overlap = jnp.clip(jnp.minimum((starts + NSA_CMP_LEN)[:, None], (sel_start + NSA_SEL_LEN)[None, :])
                       - jnp.maximum(starts[:, None], sel_start[None, :]), 0, None)
    overlap = overlap.astype(jnp.float32) / NSA_CMP_LEN
    imp = jnp.einsum('bhgtn,nj->bhtj', p_cmp, overlap)
    j = jnp.arange(nsb)[None, :]
    cb = (t // NSA_SEL_LEN)[:, None]
    forced = (j == 0) | (j == cb) | (j == cb - 1)
    score = jnp.where(j <= cb, jnp.where(forced, FORCE_SCORE, imp), NEG_INF)
    top, sel_idx = lax.top_k(score, min(NSA_SEL_COUNT, nsb))
    sel_valid = top > 0.5 * NEG_INF
    ksb = rope(k_sel).reshape(B, Hk, nsb, NSA_SEL_LEN, dh)
    vsb = v_sel.reshape(B, Hk, nsb, NSA_SEL_LEN, dh)
    o_sel = gathered_block_attention(qr, ksb, vsb, sel_idx.astype(jnp.int32), sel_valid)
    o_win, _ = banded_attention(qr, rope(k_win), v_win, NSA_WINDOW - 1)
    g = jax.nn.sigmoid(gate_logits.astype(jnp.float32)).astype(q.dtype)
    g = g.transpose(0, 2, 1, 3).reshape(B, Hk, G, T, 3)
    o = g[..., 0:1] * o_cmp + g[..., 1:2] * o_sel + g[..., 2:3] * o_win
    return o.reshape(B, Hq, T, dh)

def dilated_attention(q, k, v):
    B, H, T, dh = q.shape
    hg = C_HEADS_PER_GROUP
    outs, lses = [], []
    for gi, (w, r) in enumerate(C_GROUPS):
        L = T // r

        def strided(z):
            return z[:, gi * hg:(gi + 1) * hg].reshape(B, hg, L, r, dh).transpose(0, 1, 3, 2, 4).reshape(B, hg * r, L, dh)

        o, lse = banded_attention(strided(q)[:, :, None], strided(k), strided(v), w // r)
        outs.append(o[:, :, 0].reshape(B, hg, r, L, dh).transpose(0, 1, 3, 2, 4).reshape(B, hg, T, dh))
        lses.append(lse[:, :, 0].reshape(B, hg, r, L).transpose(0, 1, 3, 2).reshape(B, hg, T))
    wts = jax.nn.softmax(jnp.stack(lses), axis=0)
    return jnp.einsum('gbht,gbhtd->bhtd', wts.astype(q.dtype), jnp.stack(outs))

def moba_attention(q, k, v):
    B, H, T, dh = q.shape
    nb = -(-T // MOBA_BLOCK)
    padT = nb * MOBA_BLOCK - T
    kb = jnp.pad(k, ((0, 0), (0, 0), (0, padT), (0, 0))).reshape(B, H, nb, MOBA_BLOCK, dh)
    vb = jnp.pad(v, ((0, 0), (0, 0), (0, padT), (0, 0))).reshape(B, H, nb, MOBA_BLOCK, dh)
    cb = (jnp.arange(T) // MOBA_BLOCK).astype(jnp.int32)
    own = jnp.broadcast_to(cb, (B, H, T))[..., None]
    n_sel = min(MOBA_TOPK, nb - 1)
    if n_sel > 0:
        kmean = jnp.mean(kb.astype(jnp.float32), axis=3)
        gate = jnp.einsum('bhtd,bhnd->bhtn', q.astype(jnp.float32), kmean)
        past = jnp.arange(nb)[None, :] < cb[:, None]
        top, sel = lax.top_k(jnp.where(past, gate, NEG_INF), n_sel)
        idx = jnp.concatenate([sel.astype(jnp.int32), own], axis=-1)
        valid = jnp.concatenate([top > 0.5 * NEG_INF, jnp.ones_like(own, dtype=bool)], axis=-1)
    else:
        idx = own
        valid = jnp.ones_like(own, dtype=bool)
    o = gathered_block_attention(q[:, :, None], kb, vb, idx, valid)
    return o[:, :, 0]

def even_mixer(h, w_in, w_out, sinks, cmp_pe, cmp_w1, cmp_w2):
    B, T, _ = h.shape
    aq, ak, av, bq, bkc, bvc, bks, bvs, bkw, bvw, bg = split_cols(h @ w_in, EVEN_SIZES)
    ga = A_Q_HEADS // A_KV_HEADS
    qa = rope(to_heads(aq, A_Q_HEADS)).reshape(B, A_KV_HEADS, ga, T, HEAD_DIM)
    oa, _ = banded_attention(qa, rope(to_heads(ak, A_KV_HEADS)), to_heads(av, A_KV_HEADS),
                             A_WINDOW - 1, sinks.reshape(A_KV_HEADS, ga))
    oa = oa.reshape(B, A_Q_HEADS, T, HEAD_DIM)
    ob = nsa_attention(to_heads(bq, B_Q_HEADS), to_heads(bkc, B_KV_HEADS), to_heads(bvc, B_KV_HEADS),
                       to_heads(bks, B_KV_HEADS), to_heads(bvs, B_KV_HEADS),
                       to_heads(bkw, B_KV_HEADS), to_heads(bvw, B_KV_HEADS),
                       bg.reshape(B, T, B_Q_HEADS, 3), cmp_pe, cmp_w1, cmp_w2)
    return from_heads(jnp.concatenate([oa, ob], axis=1)) @ w_out

def odd_mixer(h, w_in, w_out):
    cq, ck, cv, dq, dk, dv = split_cols(h @ w_in, ODD_SIZES)
    oc = dilated_attention(rope(to_heads(cq, C_HEADS)), rope(to_heads(ck, C_HEADS)), to_heads(cv, C_HEADS))
    od = moba_attention(rope(to_heads(dq, D_HEADS)), rope(to_heads(dk, D_HEADS)), to_heads(dv, D_HEADS))
    return from_heads(jnp.concatenate([oc, od], axis=1)) @ w_out

def setup_inputs(seed: int = 0) -> dict:
    key = jax.random.key(seed)
    ks = jax.random.split(key, 16)
    f32 = jnp.float32

    def normal(k, shape, fan_in):
        return jax.random.normal(k, shape, f32) * fan_in ** -0.5

    def gain(k, shape):
        return 1.0 + 0.05 * jax.random.normal(k, shape, f32)

    return {
        "x": jax.random.normal(ks[0], (BATCH, SEQ, D_MODEL), f32),
        "ffn_norm_pre": gain(ks[1], (DEPTH, D_MODEL)),
        "mix_norm": gain(ks[2], (DEPTH, D_MODEL)),
        "ffn_norm_post": gain(ks[3], (DEPTH, D_MODEL)),
        "ffn_wi": normal(ks[4], (DEPTH, 2, D_MODEL, 2 * D_FF), D_MODEL),
        "ffn_wo": normal(ks[5], (DEPTH, 2, D_FF, D_MODEL), D_FF),
        "even_w_in": normal(ks[6], (N_EVEN, D_MODEL, EVEN_IN), D_MODEL),
        "even_w_out": normal(ks[7], (N_EVEN, EVEN_OUT, D_MODEL), EVEN_OUT),
        "even_sinks": 0.5 * jax.random.normal(ks[8], (N_EVEN, A_Q_HEADS), f32),
        "nsa_cmp_pe": 0.1 * jax.random.normal(ks[9], (N_EVEN, 2, NSA_CMP_LEN, HEAD_DIM), f32),
        "nsa_cmp_w1": normal(ks[10], (N_EVEN, 2, NSA_CMP_LEN * HEAD_DIM, NSA_CMP_HIDDEN), NSA_CMP_LEN * HEAD_DIM),
        "nsa_cmp_w2": normal(ks[11], (N_EVEN, 2, NSA_CMP_HIDDEN, HEAD_DIM), NSA_CMP_HIDDEN),
        "odd_w_in": normal(ks[12], (N_ODD, D_MODEL, ODD_IN), D_MODEL),
        "odd_w_out": normal(ks[13], (N_ODD, ODD_OUT, D_MODEL), ODD_OUT),
        "final_norm": gain(ks[14], (D_MODEL,)),
    }

def reference(x, ffn_norm_pre, mix_norm, ffn_norm_post, ffn_wi, ffn_wo, even_w_in, even_w_out,
              even_sinks, nsa_cmp_pe, nsa_cmp_w1, nsa_cmp_w2, odd_w_in, odd_w_out, final_norm):
    h = x
    for layer in range(DEPTH):
        i = layer // 2
        h = h + 0.5 * swiglu(rms_norm(h, ffn_norm_pre[layer]), ffn_wi[layer, 0], ffn_wo[layer, 0])
        hn = rms_norm(h, mix_norm[layer])
        if layer % 2 == 0:
            h = h + even_mixer(hn, even_w_in[i], even_w_out[i], even_sinks[i],
                               nsa_cmp_pe[i], nsa_cmp_w1[i], nsa_cmp_w2[i])
        else:
            h = h + odd_mixer(hn, odd_w_in[i], odd_w_out[i])
        h = h + 0.5 * swiglu(rms_norm(h, ffn_norm_post[layer]), ffn_wi[layer, 1], ffn_wo[layer, 1])
    return rms_norm(h, final_norm)


_drawn_inputs = setup_inputs


def setup_inputs(seed=0):
    import zlib

    import numpy as np

    out = dict(_drawn_inputs(seed))
    spreads = {}
    factors = {'even_sinks': 6.147}
    for name, (base, spread) in spreads.items():
        noise = np.random.default_rng([zlib.crc32(name.encode()), seed]).standard_normal(out[name].shape)
        drawn = base * np.exp(spread * noise) if base else spread * noise
        out[name] = __import__('jax').numpy.asarray(drawn.astype(out[name].dtype))
    for name, factor in factors.items():
        out[name] = (out[name] * factor).astype(out[name].dtype)
    return out
```

```python
from contextlib import ExitStack

import numpy as np

import concourse.bass as bass
from concourse import mybir

F32 = mybir.dt.float32
F32R = mybir.dt.float32r
BF16 = mybir.dt.bfloat16
I32 = mybir.dt.int32
ALU = mybir.AluOpType
ACT = mybir.ActivationFunctionType
AX = mybir.AxisListType.X

P = 128
T, DM, DFF, DH = 256, 1024, 2816, 64
TT = T // P
KT = DM // P
CF = 256
NCH = DFF // CF
UNIT = 2048
WIDE, DOWN = 512, 1024
RAW = 3
E_BLOCKS, O_BLOCKS = 4, 6
E_OUT, O_OUT = 4, 2
EPS = 1e-6
SCALE = DH ** -0.5
NEG = -1e30
CMP_LEN, CMP_STRIDE, CMP_HID = 32, 16, 256
NCMP = (T - CMP_LEN) // CMP_STRIDE + 1
NJ = CMP_LEN // 2
GATES = 24

U_F0 = 2
U_E = U_F0 + 3 * NCH
U_F1 = U_E + 2 * E_BLOCKS + E_OUT
U_F2 = U_F1 + 3 * NCH
U_O = U_F2 + 3 * NCH
U_F3 = U_O + 2 * O_BLOCKS + O_OUT
UNITS = U_F3 + 3 * NCH - 2
U_F = [U_F0, U_F1, U_F2, U_F3]
I0_F = [0, U_E + 2 * (E_BLOCKS - 1), U_F2 - 3, U_O + 2 * (O_BLOCKS - 1)]
B_E = NCH
B_F = [0, NCH + E_BLOCKS, 2 * NCH + E_BLOCKS, 3 * NCH + E_BLOCKS + O_BLOCKS]
B_O = 3 * NCH + E_BLOCKS
Q_F = [0, 2 * (NCH + E_OUT), 2 * (2 * NCH + E_OUT), 2 * (3 * NCH + E_OUT + O_OUT)]
Q_E, Q_O = 2 * NCH, 2 * (3 * NCH + E_OUT)
XS_N = [0, 4, 12, 16, 20, 26]
XS_E, XS_O = 8, 24

MASKS = {}
_at = 0
for _name, _n in (("causal0", 128), ("causal1", 256), ("band1", 256), ("dil0", 3 * 128),
                  ("dil1", 3 * 256), ("cmp0", 16), ("cmp1", 16)):
    MASKS[_name] = (_at, _at + _n)
    _at += _n
NMASK = _at
NTAB = P + 2 * TT * DH + TT * 16


def constants():
    t = np.arange(T)
    inv = 1.0 / (10000.0 ** (np.arange(0, DH, 2, dtype=np.float32) / DH))
    ang = (t[:, None].astype(np.float32) * inv[None, :]).astype(np.float32)
    cos, sin = np.cos(ang), np.sin(ang)
    rope_c = np.concatenate([cos, cos], 1).reshape(TT, P, DH)
    rope_s = np.concatenate([-sin, sin], 1).reshape(TT, P, DH)
    dist = t[:, None] - t[None, :]
    causal = dist >= 0
    band = causal & (dist <= 127)
    dil = [causal & (dist <= 128), causal & (dist % 4 == 0), causal & (dist % 16 == 0)]
    starts = np.arange(16) * CMP_STRIDE
    vis = ((starts + CMP_LEN - 1)[None, :] <= t[:, None]) & (np.arange(16) < NCMP)[None, :]
    rows = [causal[:P, :P], causal[P:], band[P:]] + [d[:P, :P] for d in dil] + [d[P:] for d in dil]
    rows += [vis[:P], vis[P:]]
    masks = np.where(np.concatenate(rows, 1), 0.0, NEG)
    tab = np.concatenate([np.eye(P), rope_c[0], rope_c[1], rope_s[0], rope_s[1],
                          vis[:P], vis[P:], masks], 1)
    return np.ascontiguousarray(tab.astype(np.float32))


def trunk(nc, x, gains, stream, gate_w, w1, w2, pe, sinks, consts, out):
    ctx = ExitStack()
    with ctx:
        def sb(name, shape, dt=F32):
            return ctx.enter_context(nc.sbuf_tensor(name, shape, dt))

        def sem(name):
            return ctx.enter_context(nc.semaphore(name))

        raw = sb("raw", [P, RAW, UNIT])
        wide_hi = sb("wide_hi", [P, 2, 2 * UNIT], F32R)
        wide_lo = sb("wide_lo", [P, 2, 2 * UNIT], F32R)
        down_hi = sb("down_hi", [P, 2, DOWN], F32R)
        down_lo = sb("down_lo", [P, 2, DOWN], F32R)
        h = sb("h", [P, TT, DM])
        xt_hi = sb("xt_hi", [P, KT, T], F32R)
        xt_lo = sb("xt_lo", [P, KT, T], F32R)
        tmp = sb("tmp", [P, TT, DM])
        silu = sb("silu", [P, TT, CF])
        ht_hi = sb("ht_hi", [P, 2, T], F32R)
        ht_lo = sb("ht_lo", [P, 2, T], F32R)
        gain = sb("gain", [P, DM])
        tab = sb("tab", [P, NTAB])
        masks = sb("masks", [P, NMASK], BF16)
        ident_b = sb("ident_b", [P, P], BF16)
        zeros_b = sb("zeros_b", [P, P], BF16)
        work = sb("work", [P, 4 * DM])
        zwork = sb("zwork", [P, 2 * DM])
        qkv = sb("qkv", [P, 6 * DM])
        gw_hi = sb("gw_hi", [P, KT, GATES], F32R)
        gw_lo = sb("gw_lo", [P, KT, GATES], F32R)
        w2k = sb("w2k", [P, 2, 2, DH])
        w2v = sb("w2v", [P, 2, DH])
        pe_t = sb("pe_t", [P, 2, NJ])
        hid = sb("hid", [P, 2, 2, 2 * NCMP])
        kc_t = sb("kc_t", [P, 2, NCMP])
        vc = sb("vc", [NCMP, 2, DH])
        sink_b = sb("sink_b", [P, 8])
        nsink = sb("nsink", [P, 8])
        stats = sb("stats", [P, 320])
        y = ctx.enter_context(nc.psum_tensor("y", [P, 4, 512], F32))
        g = [ctx.enter_context(nc.psum_tensor(f"g{i}", [P, 512], F32)) for i in range(2)]
        tp = [ctx.enter_context(nc.psum_tensor(f"tp{i}", [P, 512], F32)) for i in range(2)]

        ident = tab[:, 0:P]
        cos_t = [tab[:, P + i * DH:P + (i + 1) * DH] for i in range(TT)]
        sin_t = [tab[:, P + (TT + i) * DH:P + (TT + i + 1) * DH] for i in range(TT)]
        vis_t = [tab[:, NTAB - (TT - i) * 16:NTAB - (TT - i - 1) * 16] for i in range(TT)]
        hh = tmp[:, 0, :].rearrange("p (a t f) -> p a t f", a=2, t=TT)
        w1_slot = [work[:, s * 2 * DM:(s + 1) * 2 * DM].rearrange("p (j n) -> p j n", n=CMP_HID) for s in range(2)]
        prob = [work[:, s * DM:(s + 1) * DM] for s in range(2)]
        attn = work[:, 2 * DM:4 * DM].rearrange("p (t n) -> p t n", t=TT)
        z_t = [zwork[:, v * 512:(v + 1) * 512].rearrange("p (a t) -> p a t", a=2) for v in range(2)]
        zb = [zwork[:, DM + v * 512:DM + v * 512 + NJ * 2 * NCMP]
              .rearrange("p (j a n) -> p j a n", j=NJ, a=2) for v in range(2)]
        probt = [zwork[:, s * 512:(s + 1) * 512] for s in range(2)]
        rope_a = silu[:, :, :].rearrange("p t f -> p (t f)")
        rope_b = sb("rope_b", [P, 512])
        gw = rope_b[:, 0:KT * GATES].rearrange("p (k n) -> p k n", k=KT)

        def mask(name):
            a, b = MASKS[name]
            return masks[:, a:b]

        free = [0]

        def stat(n):
            a = free[0]
            free[0] += n
            assert free[0] <= 320
            return stats[:, a:a + n]

        ss = [[stat(1) for _ in range(TT)] for _ in range(7)]
        rstd = [[stat(1) for _ in range(TT)] for _ in range(7)]
        newton = stat(1), stat(1)
        nrstd = [stat(1) for _ in range(TT)]
        gate = [stat(GATES) for _ in range(TT)]

        raw_landed = [sem(f"raw_landed{i}") for i in range(RAW)]
        hi_done, lo_done = sem("hi_done"), sem("lo_done")
        down_used = sem("down_used")
        x_landed = [sem(f"x_landed{t}") for t in range(TT)]
        tab_landed, mask_landed, small_landed = sem("tab_landed"), sem("mask_landed"), sem("small_landed")
        gain_landed, w1_landed = sem("gain_landed"), [sem("w1_landed0"), sem("w1_landed1")]
        masks_ready, zeros_ready, nsink_ready = sem("masks_ready"), sem("zeros_ready"), sem("nsink_ready")
        gwh_ready, gwl_ready = sem("gwh_ready"), sem("gwl_ready")
        h_done, gained, ss_done, rstd_done = sem("h_done"), sem("gained"), sem("ss_done"), sem("rstd_done")
        xt_done, xh_done, xl_done = sem("xt_done"), sem("xh_done"), sem("xl_done")
        gu_done, silu_done, hh_done = sem("gu_done"), sem("silu_done"), sem("hh_done")
        ht_done, hth_done, htl_done, y0_done = sem("ht_done"), sem("hth_done"), sem("htl_done"), sem("y0_done")
        own = sem("vector_own")
        out_ready, out_landed = sem("out_ready"), sem("out_landed")
        mix = {}
        for m in ("even", "odd"):
            for n in ("proj_done", "proj_used", "rows_ready", "rows_t", "rows_copied", "scores_done",
                      "max_done", "prob_done", "pt_done", "pt_copied", "pv_done", "norm_done"):
                mix[m, n] = sem(f"{m}_{n}")
        gate_done, gate_exp, gate_ready = sem("gate_done"), sem("gate_exp"), sem("gate_ready")
        zb_ready, hid_done, hid_ready = sem("zb_ready"), sem("hid_done"), sem("hid_ready")
        cmp_done, cmp_ready, cmp_masked = sem("cmp_done"), sem("cmp_ready"), sem("cmp_masked")
        nsa_rows = sem("nsa_rows")
        sink_arg, sink_exp = sem("sink_arg"), sem("sink_exp")

        heads_q = qkv[:, 0:2 * DM].rearrange("p (a t) -> p a t", t=T)
        e_qu = qkv[:, 2 * DM:3 * DM].rearrange("p (a t) -> p a t", t=T)
        e_k = qkv[:, 3 * DM:3 * DM + 6 * T].rearrange("p (a t) -> p a t", t=T)
        e_v = qkv[:, 3 * DM + 6 * T:3 * DM + 6 * T + TT * 384].rearrange("p (t n) -> p t n", t=TT)
        o_k = qkv[:, 2 * DM:4 * DM].rearrange("p (a t) -> p a t", t=T)
        o_v = qkv[:, 4 * DM:6 * DM].rearrange("p (t n) -> p t n", t=TT)

        def make_units(m):
            units, groups = [], []
            if m == "even":
                for kind, col in (("window", 0), ("select", 512), ("wide", 512)):
                    for tt in range(TT):
                        groups.append((kind, tt, col, stat(8), stat(8), stat(8)))
                        for kv in range(2):
                            units.append((kind, tt, kv, len(groups) - 1, kv == 1))
                for tt in range(TT):
                    groups.append(("cmp", tt, 512, stat(8), stat(8), stat(8)))
                    units.append(("cmp", tt, 0, len(groups) - 1, True))
            else:
                for tt in range(TT):
                    groups.append(("odd", tt, 0, stat(8), stat(8), stat(8)))
                    for s in range(4):
                        units.append(("dilated", tt, s, len(groups) - 1, False))
                    units.append(("moba", tt, 0, len(groups) - 1, True))
            return units, groups

        UNITS_OF, GROUPS_OF = {}, {}
        for m in ("even", "odd"):
            UNITS_OF[m], GROUPS_OF[m] = make_units(m)

        def unit_halves(u):
            kind, tt, i, _, _ = u
            blocks = []
            if kind == "cmp":
                blocks = [(16 * hd, 0, hd // 4, hd * DH, True, True) for hd in range(8)]
            elif kind == "dilated":
                n = tt + 1
                for gr in range(3):
                    for kt in range(n):
                        blocks.append(((gr * n + kt) * P, kt, (gr * 4 + i) * DH, i * DH,
                                       gr == 0 and kt == 0, gr == 2 and kt == n - 1))
            else:
                for hd in range(4):
                    for kt in range(tt + 1):
                        vcol = {"window": 0, "select": 128, "wide": 256}.get(kind, 0) + i * DH
                        ocol = (4 * i + hd) * DH
                        if kind == "moba":
                            vcol, ocol = (12 + hd) * DH, (4 + hd) * DH
                        blocks.append((hd * T + kt * P, kt, vcol, ocol, kt == 0, kt == tt))
            return [blocks[a:a + 4] for a in range(0, len(blocks), 4)]

        HALF0 = {}
        for m in ("even", "odd"):
            n, HALF0[m] = 0, []
            for u in UNITS_OF[m]:
                HALF0[m].append(n)
                n += len(unit_halves(u))
            HALF0[m].append(n)

        BATCHES = {
            "even": [[(0, 4, "q", 0)], [(0, 4, "k", 0), (512, 4, "k2", 4)], [(0, 2, "v", 0)],
                     [(0, 4, "q", 4), (512, 4, "qu", 0)]],
            "odd": [[(0, 4, "q", 0)], [(0, 4, "q", 4)], [(0, 4, "ko", 0)], [(0, 4, "ko", 4)], [], []],
        }

        def batch_index(m, b, tt):
            return sum(TT * len(x) for x in BATCHES[m][:b]) + (tt * len(BATCHES[m][b]) if tt else 0)

        block = ctx.enter_context(nc.Block())


        NB = {"even": E_BLOCKS, "odd": O_BLOCKS}
        U_M = {"even": U_E, "odd": U_O}
        B_M = {"even": B_E, "odd": B_O}
        Q_M = {"even": Q_E, "odd": Q_O}
        XS_M = {"even": XS_E, "odd": XS_O}
        HALVES = {"even": 2, "odd": 1}
        U_OUT = {"even": U_E + 2 * E_BLOCKS, "odd": U_O + 2 * O_BLOCKS}
        NORM_M = {"even": 1, "odd": 4}
        NORM_F = [0, 2, 3, 5]
        Q_NORM = [0, Q_F[0] + 2 * NCH, Q_E + 2 * E_OUT, Q_F[1] + 2 * NCH, Q_F[2] + 2 * NCH,
                  Q_O + 2 * O_OUT, Q_F[3] + 2 * NCH]
        U_TAIL = [U_F[f] + 3 * NCH - 1 - (0 if f < 3 else 2) for f in range(4)]

        @block.sync
        def _(sp):
            for tt in range(TT):
                sp.dma_start(h[:, tt, :], x[tt * P:(tt + 1) * P, :]).then_inc(x_landed[tt], 16)
                if tt == 0:
                    sp.dma_start(tab[:, :], consts[:, 0:NTAB]).then_inc(tab_landed, 16)
            for s in range(RAW):
                sp.dma_start(raw[:, s, :], stream[s, :, :]).then_inc(raw_landed[s], 16)
            with sp.Fori(1, UNITS // RAW) as j:
                for s in range(RAW):
                    sp.wait_ge(lo_done, j * (2 * RAW) + 2 * (s - RAW + 1))
                    sp.dma_start(raw[:, s, :], stream[j * RAW + s, :, :]).then_inc(raw_landed[s], 16)
            for n in range(UNITS // RAW * RAW, UNITS):
                sp.wait_ge(lo_done, 2 * (n - RAW + 1))
                sp.dma_start(raw[:, n % RAW, :], stream[n, :, :]).then_inc(raw_landed[n % RAW], 16)
            for tt in range(TT):
                sp.wait_ge(out_ready, tt + 1)
                sp.dma_start(out[tt * P:(tt + 1) * P, :], tmp[:, tt, :]).then_inc(out_landed, 16)
            sp.wait_ge(out_landed, 16 * TT)

        @block.gpsimd
        def _(pool):
            pool.dma_start(gain[:, :], gains[0, :].partition_broadcast(P)).then_inc(gain_landed, 16)
            pool.dma_start(work[:, 0:NMASK], consts[:, NTAB:NTAB + NMASK]).then_inc(mask_landed, 16)
            pool.memset(zeros_b[:, :], 0.0).then_inc(zeros_ready, 1)
            pool.dma_start(gw, gate_w).then_inc(small_landed, 16)
            pool.dma_start(sink_b[:, :], sinks.partition_broadcast(P)).then_inc(small_landed, 16)
            pool.dma_start(pe_t[:, :, :], pe).then_inc(small_landed, 16)
            for d in range(2):
                pool.dma_start(w2k[:, :, d, :], w2[0]).then_inc(small_landed, 16)
            pool.dma_start(w2v[:, :, :], w2[1]).then_inc(small_landed, 16)
            pool.wait_ge(masks_ready, 2)
            for s in range(2):
                pool.dma_start(w1_slot[s], w1[s]).then_inc(w1_landed[s], 16)
            for i in range(1, 7):
                pool.wait_ge(gained, 4 * i)
                pool.dma_start(gain[:, :], gains[i, :].partition_broadcast(P)).then_inc(gain_landed, 16)
                if i == 2:
                    for s in range(2):
                        pool.wait_ge(hid_done, s + 1)
                        pool.dma_start(w1_slot[s], w1[2 + s]).then_inc(w1_landed[s], 16)

        @block.tensor
        def _(te):
            def mm(o, a, b, start=False, stop=False, **kw):
                return nc.tensor.matmul(o, a, b, start=start, stop=stop, **kw)

            def turn(o, a):
                return nc.tensor.transpose(o, a, ident)

            def wide_product(dst, tt, slot, first=None, w_hi=wide_hi, w_lo=wide_lo, n=WIDE):
                for k in range(KT):
                    if first is not None and k % 4 == 0:
                        te.wait_ge(xl_done, first + 2 * tt + k // 4 + 1)
                    xh, xl = xt_hi[:, k, tt * P:(tt + 1) * P], xt_lo[:, k, tt * P:(tt + 1) * P]
                    wh, wl = ((w[:, k, :] if slot is None else w[:, slot, k * n:(k + 1) * n])
                              for w in (w_hi, w_lo))
                    mm(dst, xh, wh, start=k == 0)
                    mm(dst, xh, wl)
                    last = mm(dst, xl, wh, stop=k == KT - 1)
                return last

            def down_product(tt, a_hi, a_lo, piece, start=False, stop=False):
                for a, w, s, e in ((a_hi, down_hi, start, False), (a_hi, down_lo, False, False),
                                   (a_lo, down_hi, False, stop)):
                    for n in range(2):
                        last = mm(y[:, 2 * tt + n, :], a, w[:, piece, n * 512:(n + 1) * 512],
                                  start=s, stop=e)
                return last

            def turn_rows(src, tt, q):
                bank = (g, tp)[tt][q]
                for k in range(4):
                    c = (4 * q + k) * P
                    last = turn(bank[:, k * P:(k + 1) * P], src[:, tt, c:c + P])
                last.then_inc(xt_done, 1)

            def norm_rows(i, tt):
                for q in range(2):
                    if i == 0 and tt == 0 and q == 0:
                        te.wait_ge(tab_landed, 16)
                    te.wait_ge(gained, 4 * i + 2 * tt + q + 1)
                    turn_rows(tmp, tt, q)

            def ffn(f):
                i = NORM_F[f]

                def gate_up(c, tt, slot):
                    if tt == 0:
                        te.wait_ge(lo_done, c * 6 + 2 * (U_F[f] - 1))
                    te.wait_ge(hh_done, c * 2 + (2 * NCH * f + tt - 1))
                    wide_product(g[tt][:, :], tt, slot).then_inc(gu_done, 1)

                def turn_products(c, par):
                    te.wait_ge(hh_done, c * 2 + (2 * NCH * f + 2))
                    for ft in range(2):
                        for tt in range(TT):
                            last = turn(tp[0][:, ft * T + tt * P:ft * T + (tt + 1) * P],
                                        hh[:, par, tt, ft * P:(ft + 1) * P])
                    last.then_inc(ht_done, 1)

                def down(c, ft, tt, stop=False):
                    return down_product(tt, ht_hi[:, ft, tt * P:(tt + 1) * P],
                                        ht_lo[:, ft, tt * P:(tt + 1) * P], ft, stop=stop)

                for tt in range(TT):
                    norm_rows(i, tt)
                    if tt == 0:
                        te.wait_ge(lo_done, 2 * (I0_F[f] + 2))
                    wide_product(g[tt][:, :], tt, B_F[f] % 2, XS_N[i]).then_inc(gu_done, 1)
                te.wait_ge(ss_done, TT * (i + 1))
                if f == 0:
                    te.wait_ge(zeros_ready, 1)
                    te.wait_ge(masks_ready, 1)
                for n in range(4):
                    last = mm(y[:, n, :], zeros_b[:, :], masks[:, 0:512], start=True)
                    if f == 0 and n >= 2:
                        last.then_inc(down_used, 1)
                with te.Fori(0, (NCH - 1) // 2) as j:
                    for v in range(2):
                        c, before = j * 2 + (1 + v), j * 2 + v
                        slot = (B_F[f] + 1 + v) % 2
                        gate_up(c, 0, slot)
                        turn_products(before, v)
                        gate_up(c, 1, slot)
                        te.wait_ge(htl_done, before + (NCH * f + 1))
                        for ft in range(2):
                            te.wait_ge(lo_done, before * 6 + (2 * (U_F[f] + 2) + ft + 1))
                            for tt in range(TT):
                                last = down(before, ft, tt)
                            last.then_inc(down_used, 1)
                c = NCH - 1
                turn_products(c, c % 2)
                te.wait_ge(htl_done, NCH * (f + 1))
                te.wait_ge(lo_done, 2 * (U_TAIL[f] + 1))
                for tt in range(TT):
                    for ft in range(2):
                        last = down(c, ft, tt, stop=ft == 1)
                        if tt == 1:
                            last.then_inc(down_used, 1)
                        elif ft == 1:
                            last.then_inc(y0_done, 1)

            def mixer(m):
                s = {n: x for (a, n), x in mix.items() if a == m}
                i = NORM_M[m]
                units, groups = UNITS_OF[m], GROUPS_OF[m]

                def turn_batches(b, tt):
                    for a, (col, count, _, _) in enumerate(BATCHES[m][b]):
                        n = batch_index(m, b, tt) + a
                        te.wait_ge(s["rows_ready"], n + 1)
                        if n >= 2:
                            te.wait_ge(s["rows_copied"], n - 1)
                        for k in range(count):
                            last = turn(tp[n % 2][:, k * P:(k + 1) * P],
                                        tmp[:, tt, col + k * P:col + (k + 1) * P])
                        last.then_inc(s["rows_t"], 1)

                def compress(v):
                    te.wait_ge(zb_ready, 2 * (v + 1))
                    for jh in range(2):
                        te.wait_ge(w1_landed[jh], 16 * (v + 1))
                        for half in range(2):
                            for j in range(NJ // 2):
                                last = mm(y[:, 2 * v + half, 0:2 * NCMP],
                                          w1_slot[jh][:, j, half * P:(half + 1) * P],
                                          zb[v][:, jh * NJ // 2 + j, :, :],
                                          start=jh == 0 and j == 0, stop=jh == 1 and j == NJ // 2 - 1)
                        last.then_inc(hid_done, 1)

                nb = NB[m]
                for b in range(nb):
                    for tt in range(TT):
                        if b == 0:
                            norm_rows(i, tt)
                        if tt == 0:
                            te.wait_ge(lo_done, 2 * (U_M[m] + 2 * b) if b else 2 * (U_M[m] - 3 + 2))
                        if b:
                            te.wait_ge(s["proj_used"], 2 * (b - 1) + tt + 1)
                        wide_product(g[tt][:, :], tt, (B_M[m] + b) % 2,
                                     XS_N[i] if b == 0 else None).then_inc(s["proj_done"], 1)
                        if b:
                            turn_batches(b - 1, tt)
                        if m == "even" and b == nb - 1 and tt == 0:
                            te.wait_ge(ss_done, TT * (i + 1))
                            compress(0)
                if m == "even":
                    te.wait_ge(gwl_ready, 1)
                    for tt in range(TT):
                        te.wait_ge(s["proj_used"], 2 * (nb - 1) + tt + 1)
                        wide_product(g[tt][:, 0:GATES], tt, None, None, gw_hi, gw_lo).then_inc(gate_done, 1)
                    compress(1)
                for tt in range(TT):
                    turn_batches(nb - 1, tt)
                if m == "even":
                    te.wait_ge(gate_exp, TT)
                    te.wait_ge(hid_ready, 2)
                    te.wait_ge(small_landed, 16 * 6)
                    for half in range(2):
                        last = mm(g[0][:, 0:2 * NCMP], w2k[:, half, :, :], hid[:, 0, half, :],
                                  start=half == 0, stop=half == 1)
                    last.then_inc(cmp_done, 1)
                    for a in range(2):
                        for half in range(2):
                            last = mm(g[1][0:NCMP, a * DH:(a + 1) * DH],
                                      hid[:, 1, half, a * NCMP:(a + 1) * NCMP], w2v[:, half, :],
                                      start=half == 0, stop=half == 1)
                    last.then_inc(cmp_done, 1)
                    te.wait_ge(cmp_ready, 2)
                te.wait_ge(ss_done, TT * (i + 1))
                te.wait_ge(s["rows_copied"], batch_index(m, nb, 0))
                te.wait_ge(s["proj_used"], 2 * nb)

                def scores(n):
                    kind, tt, a, _, _ = units[n]
                    bank, nk = y[:, 2 * (n % 2):2 * (n % 2) + 2, :], (tt + 1) * P
                    toks = slice(tt * P, (tt + 1) * P)
                    if kind == "dilated":
                        flat = bank.rearrange("p b n -> p (b n)")
                        dil = mask(f"dil{tt}")
                        off = (a % 2) * DH
                        for c in range(0, 3 * nk, 512):
                            w = min(512, 3 * nk - c)
                            mm(flat[:, c:c + w], ident_b[:, :], dil[:, c:c + w], start=True)
                            for gr in range(3):
                                if c <= gr * nk < c + w:
                                    pair = (4 * gr + a) // 2
                                    last = mm(flat[:, gr * nk:(gr + 1) * nk], heads_q[off:off + DH, pair, toks],
                                              o_k[off:off + DH, pair, 0:nk], stop=(gr + 1) * nk == c + w)
                    elif kind == "cmp":
                        for b in range(2):
                            v = bank[:, b, 0:64].rearrange("p (a n) -> p a n", a=4)
                            mm(v, ident_b[:, :], mask(f"cmp{tt}").unsqueeze(1).broadcast_to([P, 4, 16]), start=True)
                            for pos in range(4):
                                last = mm(v[:, pos, 0:NCMP], e_qu[b * DH:(b + 1) * DH, pos, toks],
                                          kc_t[b * DH:(b + 1) * DH, pos // 2, :], stop=pos == 3)
                    else:
                        mk = mask(f"causal{tt}" if tt == 0 or kind != "window" else "band1")
                        pair0 = {"window": 2 * a, "select": 4 + 2 * a, "wide": 4 + 2 * a, "moba": 6}[kind]
                        for b in range(2):
                            v = bank[:, b, :].rearrange("p (a n) -> p a n", a=2)
                            mm(v[:, :, 0:nk], ident_b[:, :], mk.unsqueeze(1).broadcast_to([P, 2, nk]), start=True)
                            for pos in range(2):
                                if kind == "moba":
                                    k = o_k[b * DH:(b + 1) * DH, 6 + pos, 0:nk]
                                else:
                                    k = e_k[b * DH:(b + 1) * DH,
                                            {"window": 0, "select": 2, "wide": 4}[kind] + a, 0:nk]
                                last = mm(v[:, pos, 0:nk], heads_q[b * DH:(b + 1) * DH, pair0 + pos, toks], k,
                                          stop=pos == 1)
                    last.then_inc(s["scores_done"], 1)

                def turn_probs(n):
                    kind = units[n][0]
                    if kind == "cmp":
                        te.wait_ge(cmp_masked, units[n][1] + 1)
                    else:
                        te.wait_ge(s["prob_done"], n + 1)
                    for a, blocks in enumerate(unit_halves(units[n])):
                        hf = HALF0[m][n] + a
                        if hf >= 2:
                            te.wait_ge(s["pt_copied"], hf - 1)
                        for k, bl in enumerate(blocks):
                            w = 16 if kind == "cmp" else P
                            last = turn(g[hf % 2][0:w, k * P:(k + 1) * P], prob[n % 2][:, bl[0]:bl[0] + w])
                        last.then_inc(s["pt_done"], 1)

                def values(n):
                    kind, tt, a, grp, _ = units[n]
                    if (n == 0 or units[n - 1][3] != grp) and grp >= 2:
                        te.wait_ge(s["norm_done"], grp - 1)
                    for a, blocks in enumerate(unit_halves(units[n])):
                        hf = HALF0[m][n] + a
                        te.wait_ge(s["pt_copied"], hf + 1)
                        for k, (_, kt, vcol, ocol, first, final) in enumerate(blocks):
                            if kind == "cmp":
                                v, w = vc[:, vcol, :], NCMP
                            else:
                                v, w = (e_v if m == "even" else o_v)[:, kt, vcol:vcol + DH], P
                            last = mm(tp[grp % 2][:, ocol:ocol + DH],
                                      probt[hf % 2][0:w, k * P:(k + 1) * P], v, start=first, stop=final)
                        last.then_inc(s["pv_done"], 1)

                scores(0)
                scores(1)
                for n in range(len(units)):
                    turn_probs(n)
                    if n + 2 < len(units):
                        scores(n + 2)
                    values(n)

                nh = HALVES[m]
                for tt in range(TT):
                    for q in range(nh):
                        if m == "even":
                            if q == 0:
                                te.wait_ge(s["norm_done"], len(groups) if tt else 1)
                            else:
                                te.wait_ge(nsa_rows, tt + 1)
                        else:
                            te.wait_ge(s["norm_done"], tt + 1)
                        turn_rows(attn, tt, q)
                pieces = 4 * nh
                u0 = U_OUT[m]

                def out_product(k, tt):
                    if k % 4 == 0:
                        te.wait_ge(xl_done, XS_M[m] + nh * tt + k // 4 + 1)
                    return down_product(tt, xt_hi[:, k, tt * P:(tt + 1) * P], xt_lo[:, k, tt * P:(tt + 1) * P],
                                        k % 2, start=k == 0, stop=k == pieces - 1)
                for k in range(pieces - 2):
                    te.wait_ge(lo_done, 2 * u0 + k + 1)
                    for tt in range(TT):
                        last = out_product(k, tt)
                    last.then_inc(down_used, 1)
                te.wait_ge(lo_done, 2 * u0 + pieces)
                for tt in range(TT):
                    for k in range(pieces - 2, pieces):
                        last = out_product(k, tt)
                        if tt == 1:
                            last.then_inc(down_used, 1)
                        elif k == pieces - 1:
                            last.then_inc(y0_done, 1)

            ffn(0)
            mixer("even")
            ffn(1)
            ffn(2)
            mixer("odd")
            ffn(3)

        @block.scalar
        def _(act):
            def copy(o, a, **kw):
                return nc.scalar.activation(o, a, ACT.Copy, **kw)

            def split_wide(c, u, part, blk):
                slot = u % RAW
                act.wait_ge(raw_landed[slot], c * 16 + 16 * (u // RAW + 1))
                copy(wide_hi[:, blk, part * UNIT:(part + 1) * UNIT], raw[:, slot, :]).then_inc(hi_done, 2)

            def split_down(c, u, q):
                slot = u % RAW
                act.wait_ge(raw_landed[slot], c * 16 + 16 * (u // RAW + 1))
                for p in range(2):
                    act.wait_ge(down_used, c * 2 + (q + p + 1))
                    copy(down_hi[:, p, :], raw[:, slot, p * DOWN:(p + 1) * DOWN]).then_inc(hi_done, 1)

            def split_rows(n, tt, q):
                act.wait_ge(xt_done, n + 1)
                copy(xt_hi[:, 4 * q:4 * q + 4, tt * P:(tt + 1) * P],
                     (g, tp)[tt][q][:, :].rearrange("p (k t) -> p k t", k=4)).then_inc(xh_done, 1)

            def norm_rows(i):
                for tt in range(TT):
                    if i < 6:
                        for q in range(2):
                            split_rows(XS_N[i] + 2 * tt + q, tt, q)
                    act.wait_ge(h_done, TT * i + tt + 1)
                    nc.scalar.activation(y[:, 2 * tt:2 * tt + 2, :], h[:, tt, :].rearrange("p (a n) -> p a n", a=2),
                                         ACT.Square, accum_out=ss[i][tt]).then_inc(ss_done, 1)

            def ffn(f):
                i = NORM_F[f]

                def silus(c, tt):
                    act.wait_ge(gu_done, c * 2 + (2 * NCH * f + tt + 1))
                    nc.scalar.activation(silu[:, tt, :], g[tt][:, 0:CF], ACT.Silu,
                                         scale=rstd[i][tt]).then_inc(silu_done, 1)

                def split_products(c):
                    act.wait_ge(ht_done, c + (NCH * f + 1))
                    copy(ht_hi[:, :, :], tp[0][:, :].rearrange("p (a t) -> p a t", a=2)).then_inc(hth_done, 1)

                def chunk(c, par, more=True):
                    split_down(c, U_F[f] - 1, Q_F[f] - 2)
                    if more:
                        act.wait_ge(gu_done, c * 2 + 2 * NCH * f)
                        split_wide(c, U_F[f], 0, (B_F[f] + par + 1) % 2)
                    silus(c, 0)
                    split_products(c - 1)
                    if more:
                        split_wide(c, U_F[f] + 1, 1, (B_F[f] + par + 1) % 2)
                    silus(c, 1)

                norm_rows(i)
                if f == 2:
                    act.wait_ge(gu_done, 2 * NCH * f)
                elif f:
                    m = "even" if f == 1 else "odd"
                    act.wait_ge(mix[m, "proj_done"], 2 * NB[m])
                for p in range(2):
                    split_wide(0, U_F[f] + p, p, (B_F[f] + 1) % 2)
                for tt in range(TT):
                    act.wait_ge(rstd_done, TT * i + tt + 1)
                    silus(0, tt)
                pairs = (NCH - 1) // 2
                with act.Fori(0, pairs if f < 3 else pairs - 1) as j:
                    for v in range(2):
                        chunk(j * 2 + (1 + v), 1 + v)
                if f == 3:
                    chunk(NCH - 2, (NCH - 2) % 2)
                    chunk(NCH - 1, (NCH - 1) % 2, more=False)
                split_down(0, U_TAIL[f], Q_F[f] + 2 * (NCH - 1))
                split_products(NCH - 1)

            def mixer(m):
                s = {n: x for (a, n), x in mix.items() if a == m}
                i, nb, units = NORM_M[m], NB[m], UNITS_OF[m]

                def copy_batches(b, tt):
                    toks = slice(tt * P, (tt + 1) * P)
                    for a, (_, count, kind, at) in enumerate(BATCHES[m][b]):
                        n = batch_index(m, b, tt) + a
                        act.wait_ge(s["rows_t"], n + 1)
                        bank = tp[n % 2][:, :].rearrange("p (k t) -> p k t", k=4)
                        if kind == "q":
                            last = copy(heads_q[:, at:at + 4, toks], bank)
                        elif kind == "qu":
                            last = copy(e_qu[:, :, toks], bank)
                        elif kind == "ko":
                            last = copy(o_k[:, at:at + 4, toks], bank)
                        elif kind == "k":
                            last = copy(e_k[:, 0:4, toks], bank)
                        else:
                            z, src = (z_t[0], bank[:, 2:4, :]) if kind == "k2" else (z_t[1], bank[:, 0:2, :])
                            if kind == "k2":
                                copy(e_k[:, 4:6, toks], bank[:, 0:2, :])
                            copy(z[0:DH, :, toks], src[0:DH, :, :])
                            lo = 1 if tt == 0 else 0
                            last = copy(z[DH:P, :, tt * P + lo - 1:(tt + 1) * P - 1], src[DH:P, :, lo:P])
                        last.then_inc(s["rows_copied"], 1)

                def gelu(v):
                    act.wait_ge(hid_done, 2 * v + 2)
                    nc.scalar.activation(hid[:, v, :, :], y[:, 2 * v:2 * v + 2, 0:2 * NCMP],
                                         ACT.Gelu_apprx_tanh).then_inc(hid_ready, 1)

                norm_rows(i)
                for b in range(nb):
                    if b == 0:
                        act.wait_ge(gu_done, 2 * NCH * (1 if m == "even" else 3))
                    else:
                        act.wait_ge(s["proj_done"], 2 * b)
                    for p in range(TT):
                        split_wide(0, U_M[m] + 2 * b + p, p, (B_M[m] + b + 1) % 2)
                        if b:
                            copy_batches(b - 1, p)
                if m == "even":
                    gelu(0)
                    for tt in range(TT):
                        act.wait_ge(gate_done, tt + 1)
                        act.wait_ge(rstd_done, TT * i + tt + 1)
                        nc.scalar.activation(gate[tt], g[tt][:, 0:GATES], ACT.Exp,
                                             scale=nrstd[tt]).then_inc(gate_exp, 1)
                    gelu(1)
                for tt in range(TT):
                    copy_batches(nb - 1, tt)
                if m == "even":
                    act.wait_ge(cmp_done, 1)
                    copy(kc_t[:, :, :], g[0][:, 0:2 * NCMP].rearrange("p (a n) -> p a n", a=2)).then_inc(cmp_ready, 1)
                    act.wait_ge(cmp_done, 2)
                    copy(vc[:, :, :], g[1][0:NCMP, 0:2 * DH].rearrange("p (a n) -> p a n", a=2)).then_inc(cmp_ready, 1)
                split_down(0, U_OUT[m], Q_M[m])
                for n, (kind, tt, a, grp, final) in enumerate(units):
                    nk = (tt + 1) * P
                    _, _, _, nmax, den, r = GROUPS_OF[m][grp]
                    act.wait_ge(s["max_done"], n + 1)
                    if n >= 2:
                        act.wait_ge(s["pt_done"], HALF0[m][n - 1])
                    bank = y[:, 2 * (n % 2):2 * (n % 2) + 2, :]
                    if kind == "dilated":
                        last = nc.scalar.activation(prob[n % 2][:, 0:3 * nk],
                                                    bank.rearrange("p b n -> p (b n)")[:, 0:3 * nk], ACT.Exp,
                                                    bias=nmax[:, a:a + 1], scale=SCALE, accum_out=den[:, a:a + 1])
                    elif kind == "cmp":
                        last = nc.scalar.activation(prob[n % 2][:, 0:P], prob[n % 2][:, 0:P], ACT.Exp, scale=SCALE)
                    else:
                        for hd in range(4):
                            c = 4 * a + hd + (4 if kind == "moba" else 0)
                            last = nc.scalar.activation(prob[n % 2][:, hd * T:hd * T + nk],
                                                        bank[:, hd % 2, (hd // 2) * T:(hd // 2) * T + nk], ACT.Exp,
                                                        bias=nmax[:, c:c + 1], scale=SCALE,
                                                        accum_out=den[:, c:c + 1])
                    last.then_inc(s["prob_done"], 1)
                    if kind == "window" and final:
                        act.wait_ge(sink_arg, tt + 1)
                        nc.scalar.activation(r, r, ACT.Exp).then_inc(sink_exp, 1)
                for tt in range(TT):
                    for q in range(HALVES[m]):
                        split_rows(XS_M[m] + HALVES[m] * tt + q, tt, q)
                for b in range(1, 2 * HALVES[m]):
                    split_down(0, U_OUT[m] + b, Q_M[m] + 2 * b)

            for n in range(2):
                split_wide(0, n, n, 0)
            act.wait_ge(small_landed, 16 * 6)
            copy(gw_hi[:, :, :], gw).then_inc(gwh_ready, 1)
            ffn(0)
            mixer("even")
            ffn(1)
            ffn(2)
            mixer("odd")
            ffn(3)
            norm_rows(6)

        @block.vector
        def _(dve):
            count = [0]

            def link(ins):
                count[0] += 1
                ins.then_inc(own, 1)

            def settle():
                dve.wait_ge(own, count[0])

            tt_op, ts_op, stt = nc.vector.tensor_tensor, nc.vector.tensor_scalar, nc.vector.scalar_tensor_tensor

            def split_wide(c, u, part, blk):
                dve.wait_ge(hi_done, c * 6 + 2 * (u + 1))
                w = slice(part * UNIT, (part + 1) * UNIT)
                tt_op(wide_lo[:, blk, w], raw[:, u % RAW, :], wide_hi[:, blk, w].bitcast(F32),
                      ALU.subtract).then_inc(lo_done, 2)

            def split_down(c, u):
                for p in range(2):
                    dve.wait_ge(hi_done, c * 6 + (2 * u + p + 1))
                    tt_op(down_lo[:, p, :], raw[:, u % RAW, p * DOWN:(p + 1) * DOWN],
                          down_hi[:, p, :].bitcast(F32), ALU.subtract).then_inc(lo_done, 1)

            def split_rows(n, tt, q):
                dve.wait_ge(xh_done, n + 1)
                w = (slice(None), slice(4 * q, 4 * q + 4), slice(tt * P, (tt + 1) * P))
                tt_op(xt_lo[w], (g, tp)[tt][q][:, :].rearrange("p (k t) -> p k t", k=4),
                      xt_hi[w].bitcast(F32), ALU.subtract).then_inc(xl_done, 1)

            def inverse_root(r, v):
                a, b = newton
                link(ts_op(v, v, 1.0 / DM, EPS, ALU.mult, ALU.add))
                settle()
                link(ts_op(r.bitcast(I32), v.bitcast(I32), -0.5, float(0x5F3759DF), ALU.mult, ALU.add))
                for step in range(3):
                    settle()
                    link(stt(a, r, v, r, ALU.mult, ALU.mult))
                    settle()
                    link(ts_op(b, a, -0.5, 1.5, ALU.mult, ALU.add))
                    settle()
                    last = tt_op(r, r, b, ALU.mult)
                    if step < 2:
                        link(last)
                return last

            def norm_rows(i):
                for tt in range(TT):
                    if i == 0:
                        dve.wait_ge(x_landed[tt], 16)
                        dve.sem_inc(h_done, 1)
                    else:
                        if tt == 0:
                            dve.wait_ge(y0_done, i)
                        else:
                            dve.wait_ge(down_used, 2 + Q_NORM[i])
                        for q in range(2):
                            hq = h[:, tt, q * 512:(q + 1) * 512]
                            ins = stt(hq, y[:, 2 * tt + q, :], 1.0 if i in (2, 5) else 0.5, hq, ALU.mult, ALU.add)
                            if q == 0:
                                link(ins)
                            else:
                                ins.then_inc(h_done, 1)
                    if tt == 0:
                        dve.wait_ge(gain_landed, 16 * (i + 1))
                    if i < 6:
                        for q in range(2):
                            w = slice(q * 512, (q + 1) * 512)
                            if q == 0:
                                settle()
                            elif i:
                                dve.wait_ge(h_done, TT * i + tt + 1)
                            tt_op(tmp[:, tt, w], h[:, tt, w], gain[:, w], ALU.mult).then_inc(gained, 1)
                        for q in range(2):
                            split_rows(XS_N[i] + 2 * tt + q, tt, q)
                    dve.wait_ge(ss_done, TT * i + tt + 1)
                    inverse_root(rstd[i][tt], ss[i][tt]).then_inc(rstd_done, 1)
                    if i == 1:
                        dve.wait_ge(rstd_done, TT * i + tt + 1)
                        link(ts_op(nrstd[tt], rstd[i][tt], -1.0, None, ALU.mult))
                    if i == 6:
                        dve.wait_ge(rstd_done, TT * i + tt + 1)
                        stt(tmp[:, tt, :], h[:, tt, :], rstd[i][tt], gain[:, :], ALU.mult,
                            ALU.mult).then_inc(out_ready, 1)

            def ffn(f):
                i = NORM_F[f]

                def products(c, tt, par):
                    dve.wait_ge(silu_done, c * 2 + (2 * NCH * f + tt + 1))
                    stt(hh[:, par, tt, :], g[tt][:, CF:2 * CF], rstd[i][tt], silu[:, tt, :], ALU.mult,
                        ALU.mult).then_inc(hh_done, 1)

                def split_products(c):
                    dve.wait_ge(hth_done, c + (NCH * f + 1))
                    tt_op(ht_lo[:, :, :], tp[0][:, :].rearrange("p (a t) -> p a t", a=2),
                          ht_hi[:, :, :].bitcast(F32), ALU.subtract).then_inc(htl_done, 1)

                def chunk(c, par, more=True):
                    split_down(c, U_F[f] - 1)
                    if more:
                        split_wide(c, U_F[f], 0, (B_F[f] + par + 1) % 2)
                    products(c, 0, par % 2)
                    split_products(c - 1)
                    if more:
                        split_wide(c, U_F[f] + 1, 1, (B_F[f] + par + 1) % 2)
                    products(c, 1, par % 2)

                norm_rows(i)
                for p in range(2):
                    split_wide(0, U_F[f] + p, p, (B_F[f] + 1) % 2)
                for tt in range(TT):
                    products(0, tt, 0)
                pairs = (NCH - 1) // 2
                with dve.Fori(0, pairs if f < 3 else pairs - 1) as j:
                    for v in range(2):
                        chunk(j * 2 + (1 + v), 1 + v)
                if f == 3:
                    chunk(NCH - 2, (NCH - 2) % 2)
                    chunk(NCH - 1, (NCH - 1) % 2, more=False)
                split_down(0, U_TAIL[f])
                split_products(NCH - 1)

            def mixer(m):
                s = {n: x for (a, n), x in mix.items() if a == m}
                i, nb, units, groups = NORM_M[m], NB[m], UNITS_OF[m], GROUPS_OF[m]

                def rotate(tt, n):
                    v = g[tt][:, 0:n * DH].rearrange("p (a d) -> p a d", d=DH)
                    ra = rope_a[:, 0:n * DH].rearrange("p (a d) -> p a d", d=DH)
                    rb = rope_b[:, 0:n * DH].rearrange("p (a d) -> p a d", d=DH)
                    r, hd = rstd[i][tt], DH // 2
                    link(stt(ra, v, r, cos_t[tt].unsqueeze(1).broadcast_to([P, n, DH]), ALU.mult, ALU.mult))
                    link(stt(rb[:, :, 0:hd], v[:, :, hd:DH], r,
                             sin_t[tt][:, 0:hd].unsqueeze(1).broadcast_to([P, n, hd]), ALU.mult, ALU.mult))
                    return ra, rb, stt(rb[:, :, hd:DH], v[:, :, 0:hd], r,
                                       sin_t[tt][:, hd:DH].unsqueeze(1).broadcast_to([P, n, hd]), ALU.mult, ALU.mult)

                def leave(b, tt):
                    used = 2 * b + tt + 1
                    dve.wait_ge(s["proj_done"], used)
                    kinds = BATCHES[m][b]
                    before = batch_index(m, b - 1, tt) + len(BATCHES[m][b - 1]) if b else 0
                    if kinds and before:
                        dve.wait_ge(s["rows_t"], before)
                    rows, bank = tmp[:, tt, :], g[tt]
                    done = batch_index(m, b, tt)
                    if kinds and done:
                        dve.wait_ge(s["rows_ready"], done)
                    if m == "odd" and b >= 4:
                        ts_op(o_v[:, tt, (b - 4) * 512:(b - 3) * 512], bank[:, :], rstd[i][tt], None,
                              ALU.mult).then_inc(s["proj_used"], 1)
                    elif m == "even" and b == 1:
                        ra, rb, last = rotate(tt, 6)
                        link(last)
                        v = bank[:, 6 * DH:8 * DH].rearrange("p (a d) -> p a d", d=DH)
                        for d in range(2):
                            last = ts_op(rows[:, 768:1024].rearrange("p (a e d) -> p a e d", a=2, e=2)[:, :, d, :],
                                         v, rstd[i][tt], None, ALU.mult)
                            if d == 0:
                                link(last)
                        last.then_inc(s["proj_used"], 1)
                        settle()
                        dve.wait_ge(s["proj_used"], used)
                        r4 = rows[:, 0:768].rearrange("p (a e d) -> p a e d", a=6, e=2)
                        link(tt_op(r4[:, :, 0, :], ra, rb, ALU.add))
                        settle()
                        tt_op(r4[:, :, 1, :], ra, rb, ALU.add).then_inc(s["rows_ready"], 2)
                    elif m == "even" and b == 2:
                        link(ts_op(e_v[:, tt, :], bank[:, 0:384], rstd[i][tt], None, ALU.mult))
                        v = bank[:, 6 * DH:8 * DH].rearrange("p (a d) -> p a d", d=DH)
                        for d in range(2):
                            last = ts_op(rows[:, 0:256].rearrange("p (a e d) -> p a e d", a=2, e=2)[:, :, d, :],
                                         v, rstd[i][tt], None, ALU.mult)
                            if d == 0:
                                link(last)
                        last.then_inc(s["proj_used"], 1)
                        dve.wait_ge(s["proj_used"], used)
                        dve.sem_inc(s["rows_ready"], 1)
                    else:
                        if m == "even" and b == 3:
                            link(ts_op(rows[:, 512:1024], bank[:, :], rstd[i][tt], None, ALU.mult))
                        ra, rb, last = rotate(tt, 8)
                        last.then_inc(s["proj_used"], 1)
                        settle()
                        dve.wait_ge(s["proj_used"], used)
                        tt_op(rows[:, 0:512].rearrange("p (a d) -> p a d", d=DH), ra, rb,
                              ALU.add).then_inc(s["rows_ready"], len(kinds))

                def windows(v):
                    dve.wait_ge(s["rows_copied"], batch_index(m, 2 + v, 0))
                    z = z_t[v][:, :, :]
                    for a in range(2):
                        sa = bass.AP(tensor=z.tensor, offset=z.offset + a * T,
                                     ap=[list(z.ap[0]), [2, NJ], [CMP_STRIDE, NCMP]])
                        last = tt_op(zb[v][:, :, a, :], sa,
                                     pe_t[:, v, :].unsqueeze(2).broadcast_to([P, NJ, NCMP]), ALU.add)
                        last.then_inc(zb_ready, 1)

                norm_rows(i)
                if m == "even":
                    dve.wait_ge(small_landed, 16 * 6)
                for b in range(nb):
                    for p in range(TT):
                        split_wide(0, U_M[m] + 2 * b + p, p, (B_M[m] + b + 1) % 2)
                        if m == "even" and b == nb - 1 and p == 0:
                            windows(0)
                        leave(b, p)
                if m == "even":
                    windows(1)
                    for tt in range(TT):
                        dve.wait_ge(gate_exp, tt + 1)
                        link(ts_op(gate[tt], gate[tt], 1.0, None, ALU.add))
                        settle()
                        link(nc.vector.reciprocal(gate[tt], gate[tt]))
                split_down(0, U_OUT[m])

                def maxima(n):
                    kind, tt, a, grp, final = units[n]
                    nk = (tt + 1) * P
                    _, _, _, nmax, den, r = groups[grp]
                    bank = y[:, 2 * (n % 2):2 * (n % 2) + 2, :]
                    dve.wait_ge(s["scores_done"], n + 1)
                    if kind == "dilated":
                        w = slice(a, a + 1)
                        link(nc.vector.reduce_max(nmax[:, w], bank.rearrange("p b n -> p (b n)")[:, 0:3 * nk], AX))
                    elif kind == "cmp":
                        v = bank[:, :, 0:64].rearrange("p b (a n) -> p b a n", a=4)
                        mx = nmax[:, :].rearrange("p (a b) -> p b a", b=2)
                        link(nc.vector.reduce_max(mx, v, AX))
                        settle()
                        if n >= 2:
                            dve.wait_ge(s["pt_done"], HALF0[m][n - 1])
                        pv = prob[n % 2][:, 0:P].rearrange("p (a b n) -> p b a n", b=2, n=16)
                        link(tt_op(pv[:, 0], v[:, 0], mx[:, 0, :].unsqueeze(2).broadcast_to([P, 4, 16]), ALU.subtract))
                        settle()
                        tt_op(pv[:, 1], v[:, 1], mx[:, 1, :].unsqueeze(2).broadcast_to([P, 4, 16]),
                              ALU.subtract).then_inc(s["max_done"], 1)
                        return
                    else:
                        c = 4 * a + (4 if kind == "moba" else 0)
                        w = slice(c, c + 4)
                        v = bank.rearrange("p b (a n) -> p b a n", a=2)[:, :, :, 0:nk]
                        link(nc.vector.reduce_max(nmax[:, w].rearrange("p (a b) -> p b a", b=2), v, AX))
                    settle()
                    if kind == "window":
                        stt(nmax[:, w], nmax[:, w], -SCALE, nsink[:, w], ALU.mult, ALU.min).then_inc(s["max_done"], 1)
                        if final:
                            dve.wait_ge(s["max_done"], n + 1)
                            tt_op(r, sink_b[:, :], nmax, ALU.add).then_inc(sink_arg, 1)
                    else:
                        ts_op(nmax[:, w], nmax[:, w], -SCALE, None, ALU.mult).then_inc(s["max_done"], 1)

                def cmp_sum(n):
                    _, tt, _, grp, _ = units[n]
                    den = groups[grp][4]
                    dve.wait_ge(s["prob_done"], n + 1)
                    pv = prob[n % 2][:, 0:P].rearrange("p (a n) -> p a n", n=16)
                    link(tt_op(pv, pv, vis_t[tt].unsqueeze(1).broadcast_to([P, 8, 16]), ALU.mult))
                    settle()
                    link(nc.vector.reduce_sum(den, pv, AX))
                    settle()
                    stt(den, den, 0.0, den, ALU.is_le, ALU.add).then_inc(cmp_masked, 1)

                def copy_probs(n):
                    w = 16 if units[n][0] == "cmp" else P
                    for a, blocks in enumerate(unit_halves(units[n])):
                        hf = HALF0[m][n] + a
                        c = slice(0, len(blocks) * P)
                        dve.wait_ge(s["pt_done"], hf + 1)
                        if hf >= 2:
                            dve.wait_ge(s["pv_done"], hf - 1)
                        nc.vector.tensor_copy(probt[hf % 2][0:w, c], g[hf % 2][0:w, c]).then_inc(s["pt_copied"], 1)

                def normalise(grp, hf):
                    kind, tt, col, nmax, den, r = groups[grp]
                    if kind == "window":
                        dve.wait_ge(sink_exp, tt + 1)
                        link(tt_op(den, den, r, ALU.add))
                        settle()
                    link(nc.vector.reciprocal(r, den))
                    settle()
                    if kind in ("select", "wide", "cmp"):
                        ch = {"cmp": 0, "select": 1, "wide": 2}[kind]
                        link(tt_op(r, r, gate[tt].rearrange("p (a c) -> p c a", c=3)[:, ch, :], ALU.mult))
                        settle()
                    dve.wait_ge(s["pv_done"], hf)
                    o = tp[grp % 2][:, :].rearrange("p (a d) -> p a d", d=DH)
                    rb = r.unsqueeze(2).broadcast_to([P, 8, DH])
                    rows = attn[:, tt, col:col + 512].rearrange("p (a d) -> p a d", d=DH)
                    if kind in ("wide", "cmp"):
                        part = rope_a.rearrange("p (a d) -> p a d", d=DH)
                        tt_op(part, o, rb, ALU.mult).then_inc(s["norm_done"], 1)
                        dve.wait_ge(s["norm_done"], grp + 1)
                        last = tt_op(rows, rows, part, ALU.add)
                        if kind == "cmp":
                            last.then_inc(nsa_rows, 1)
                        else:
                            link(last)
                            settle()
                    else:
                        tt_op(rows, o, rb, ALU.mult).then_inc(s["norm_done"], 1)

                maxima(0)
                maxima(1)
                for n, u in enumerate(units):
                    if u[0] == "cmp":
                        cmp_sum(n)
                        dve.wait_ge(cmp_masked, u[1] + 1)
                    copy_probs(n)
                    if n + 2 < len(units):
                        maxima(n + 2)
                    if u[4]:
                        normalise(u[3], HALF0[m][n + 1])
                for tt in range(TT):
                    for q in range(HALVES[m]):
                        split_rows(XS_M[m] + HALVES[m] * tt + q, tt, q)
                for b in range(1, 2 * HALVES[m]):
                    split_down(0, U_OUT[m] + b)

            dve.wait_ge(tab_landed, 16)
            dve.wait_ge(mask_landed, 16)
            nc.vector.tensor_copy(masks[:, :], work[:, 0:NMASK]).then_inc(masks_ready, 1)
            nc.vector.tensor_copy(ident_b[:, :], ident).then_inc(masks_ready, 1)
            for n in range(2):
                split_wide(0, n, n, 0)
            dve.wait_ge(small_landed, 16 * 6)
            link(ts_op(nsink[:, :], sink_b[:, :], -1.0, None, ALU.mult))
            dve.wait_ge(gwh_ready, 1)
            tt_op(gw_lo[:, :, :], gw, gw_hi[:, :, :].bitcast(F32), ALU.subtract).then_inc(gwl_ready, 1)
            ffn(0)
            mixer("even")
            ffn(1)
            ffn(2)
            mixer("odd")
            ffn(3)
            norm_rows(6)


def kernel(**inputs):
    from concourse import bacc
    from concourse.bass_utils import run_bass_kernel_spmd

    a = {k: np.asarray(v) for k, v in inputs.items()}

    def wide_ffn(wi):
        v = wi.reshape(KT, P, 2, NCH, CF).transpose(3, 1, 0, 2, 4)
        return [c.reshape(P, 2, UNIT).transpose(1, 0, 2) for c in v]

    def wide_in(w):
        v = w.reshape(KT, P, -1, WIDE).transpose(2, 1, 0, 3)
        return [c.reshape(P, 2, UNIT).transpose(1, 0, 2) for c in v]

    def down_blocks(w):
        return [c.transpose(1, 0, 2).reshape(1, P, UNIT) for c in w.reshape(-1, 2, P, DOWN)]

    ew = a["even_w_in"][0]
    cols = {}
    at = 0
    for name, n in (("aq", 512), ("ak", 128), ("av", 128), ("bq", 512), ("kc", 128), ("vc", 128),
                    ("ks", 128), ("vs", 128), ("kw", 128), ("vw", 128), ("bg", GATES)):
        cols[name] = ew[:, at:at + n]
        at += n
    order = ("aq", "ak", "ks", "kw", "kc", "av", "vs", "vw", "vc", "bq")
    even_in = wide_in(np.concatenate([cols[n] for n in order], axis=1))
    ow = a["odd_w_in"][0]
    o = [ow[:, 0:768], ow[:, 768:1536], ow[:, 1536:2304], ow[:, 2304:2560], ow[:, 2560:2816], ow[:, 2816:3072]]
    odd_in = wide_in(np.concatenate([o[0], o[3], o[1], o[4], o[2], o[5]], axis=1))
    even_out, odd_out = down_blocks(a["even_w_out"][0]), down_blocks(a["odd_w_out"][0])
    ffns = [(wide_ffn(a["ffn_wi"][layer, s]), down_blocks(a["ffn_wo"][layer, s])) for layer in range(2) for s in range(2)]

    units = [ffns[0][0][0]]

    def ffn_units(f, following):
        wide, down = ffns[f]
        wide = wide + following
        for c in range(NCH):
            if c:
                units.append(down[c - 1])
            if c + 1 < len(wide):
                units.append(wide[c + 1])
        units.append(down[-1])

    ffn_units(0, even_in[:1])
    units += even_in[1:] + [ffns[1][0][0]] + even_out
    ffn_units(1, ffns[2][0][:1])
    ffn_units(2, odd_in[:1])
    units += odd_in[1:] + [ffns[3][0][0]] + odd_out
    ffn_units(3, [])
    stream = np.concatenate(units)
    assert stream.shape == (UNITS, P, UNIT)

    gains = np.stack([a["ffn_norm_pre"][0], a["mix_norm"][0], a["ffn_norm_post"][0],
                      a["ffn_norm_pre"][1], a["mix_norm"][1], a["ffn_norm_post"][1], a["final_norm"]])
    w1 = a["nsa_cmp_w1"][0].reshape(2, 2, NJ // 2, P, CMP_HID).transpose(0, 1, 3, 2, 4).reshape(4, P, NJ // 2, CMP_HID)
    arrays = {
        "x": a["x"][0],
        "gains": gains,
        "stream": stream,
        "gate_w": cols["bg"].reshape(KT, P, GATES).transpose(1, 0, 2),
        "w1": w1,
        "w2": a["nsa_cmp_w2"][0].reshape(2, 2, P, DH).transpose(0, 2, 1, 3),
        "pe": a["nsa_cmp_pe"][0].reshape(2, NJ, P).transpose(2, 0, 1),
        "sinks": a["even_sinks"][0],
        "consts": constants(),
    }
    arrays = {k: np.ascontiguousarray(v) for k, v in arrays.items()}
    nc = bacc.Bacc("TRN2", target_bir_lowering=False, num_devices=1)
    aps = [nc.dram_tensor(n, v.shape, F32, kind="ExternalInput").ap() for n, v in arrays.items()]
    out = nc.dram_tensor("out", (T, DM), F32, kind="ExternalOutput").ap()
    trunk(nc, *aps, out)
    r = run_bass_kernel_spmd(nc, [arrays], core_ids=[0])
    return r.results[0]["out"].reshape(1, T, DM)
```

```python
from contextlib import ExitStack

import numpy as np

import concourse.bass as bass
from concourse import mybir

F32 = mybir.dt.float32
F32R = mybir.dt.float32r
BF16 = mybir.dt.bfloat16
I32 = mybir.dt.int32
ALU = mybir.AluOpType
ACT = mybir.ActivationFunctionType
AX = mybir.AxisListType.X

P = 128
T, DM, DFF, DH = 256, 1024, 2816, 64
TT = T // P
KT = DM // P
CF = 256
NCH = DFF // CF
UNIT = 2048
WIDE, DOWN = 512, 1024
RAW = 3
E_BLOCKS, O_BLOCKS = 4, 6
E_OUT, O_OUT = 4, 2
EPS = 1e-6
SCALE = DH ** -0.5
NEG = -1e30
CMP_LEN, CMP_STRIDE, CMP_HID = 32, 16, 256
NCMP = (T - CMP_LEN) // CMP_STRIDE + 1
NJ = CMP_LEN // 2
GATES = 24

U_F0 = 2
U_E = U_F0 + 3 * NCH
U_F1 = U_E + 2 * E_BLOCKS + E_OUT
U_F2 = U_F1 + 3 * NCH
U_O = U_F2 + 3 * NCH
U_F3 = U_O + 2 * O_BLOCKS + O_OUT
UNITS = U_F3 + 3 * NCH - 2
U_F = [U_F0, U_F1, U_F2, U_F3]
I0_F = [0, U_E + 2 * (E_BLOCKS - 1), U_F2 - 3, U_O + 2 * (O_BLOCKS - 1)]
B_E = NCH
B_F = [0, NCH + E_BLOCKS, 2 * NCH + E_BLOCKS, 3 * NCH + E_BLOCKS + O_BLOCKS]
B_O = 3 * NCH + E_BLOCKS
D_F0 = 2
D_E = D_F0 + 2 * (NCH - 1)
D_F1 = D_E + 2
D_F2 = D_F1 + 2 * (NCH - 1)
D_O = D_F2 + 2 * (NCH - 1)
D_F3 = D_O + 2
D_F = [D_F0, D_F1, D_F2, D_F3]
XS_N = [0, 4, 12, 16, 20, 26]
XS_E, XS_O = 8, 24

MASKS = {}
_at = 0
for _name, _n in (("causal0", 128), ("causal1", 256), ("band1", 256), ("dil0", 3 * 128),
                  ("dil1", 3 * 256), ("cmp0", 16), ("cmp1", 16)):
    MASKS[_name] = (_at, _at + _n)
    _at += _n
NMASK = _at
NTAB = P + 2 * TT * DH + 8 + TT * 16


def constants():
    t = np.arange(T)
    inv = 1.0 / (10000.0 ** (np.arange(0, DH, 2, dtype=np.float32) / DH))
    ang = (t[:, None].astype(np.float32) * inv[None, :]).astype(np.float32)
    cos, sin = np.cos(ang), np.sin(ang)
    rope_c = np.concatenate([cos, cos], 1).reshape(TT, P, DH)
    rope_s = np.concatenate([-sin, sin], 1).reshape(TT, P, DH)
    dist = t[:, None] - t[None, :]
    causal = dist >= 0
    band = causal & (dist <= 127)
    dil = [causal & (dist <= 128), causal & (dist % 4 == 0), causal & (dist % 16 == 0)]
    starts = np.arange(16) * CMP_STRIDE
    vis = ((starts + CMP_LEN - 1)[None, :] <= t[:, None]) & (np.arange(16) < NCMP)[None, :]
    rows = [causal[:P, :P], causal[P:], band[P:]] + [d[:P, :P] for d in dil] + [d[P:] for d in dil]
    rows += [vis[:P], vis[P:]]
    masks = np.where(np.concatenate(rows, 1), 0.0, NEG)
    own = (np.arange(P)[:, None] // 16 == np.arange(8)[None, :]) & (np.arange(P)[:, None] % 16 < NCMP)
    tab = np.concatenate([np.eye(P), rope_c[0], rope_c[1], rope_s[0], rope_s[1], own,
                          vis[:P], vis[P:], masks], 1)
    return np.ascontiguousarray(tab.astype(np.float32))


def trunk(nc, x, gains, stream, gate_w, w1, w2, pe, sinks, consts, out):
    ctx = ExitStack()
    with ctx:
        def sb(name, shape, dt=F32):
            return ctx.enter_context(nc.sbuf_tensor(name, shape, dt))

        def sem(name):
            return ctx.enter_context(nc.semaphore(name))

        raw = sb("raw", [P, RAW, UNIT])
        wide_hi = sb("wide_hi", [P, 2, 2 * UNIT], F32R)
        wide_lo = sb("wide_lo", [P, 2, 2 * UNIT], F32R)
        down_hi = sb("down_hi", [P, 2, DOWN], F32R)
        down_lo = sb("down_lo", [P, 2, DOWN], F32R)
        h = sb("h", [P, TT, DM])
        xt_hi = sb("xt_hi", [P, KT, T], F32R)
        xt_lo = sb("xt_lo", [P, KT, T], F32R)
        tmp = sb("tmp", [P, TT, DM])
        silu = sb("silu", [P, TT, CF])
        ht_hi = sb("ht_hi", [P, 2, T], F32R)
        ht_lo = sb("ht_lo", [P, 2, T], F32R)
        gain = sb("gain", [P, DM])
        tab = sb("tab", [P, NTAB])
        masks = sb("masks", [P, NMASK], BF16)
        ident_b = sb("ident_b", [P, P], BF16)
        zeros_b = sb("zeros_b", [P, 512], BF16)
        work = sb("work", [P, 4 * DM])
        zwork = sb("zwork", [P, 2 * DM])
        qkv = sb("qkv", [P, 6 * DM])
        gw_hi = sb("gw_hi", [P, KT, GATES], F32R)
        gw_lo = sb("gw_lo", [P, KT, GATES], F32R)
        w2k = sb("w2k", [P, 2, 2, DH])
        w2v = sb("w2v", [P, 2, DH])
        pe_t = sb("pe_t", [P, 2, NJ])
        sink_b = sb("sink_b", [P, 8])
        nsink = sb("nsink", [P, 8])
        stats = sb("stats", [P, 320])
        y = ctx.enter_context(nc.psum_tensor("y", [P, 4, 512], F32))
        g = [ctx.enter_context(nc.psum_tensor(f"g{i}", [P, 512], F32)) for i in range(2)]
        tp = [ctx.enter_context(nc.psum_tensor(f"tp{i}", [P, 512], F32)) for i in range(2)]

        ident = tab[:, 0:P]
        cos_t = [tab[:, P + i * DH:P + (i + 1) * DH] for i in range(TT)]
        sin_t = [tab[:, P + (TT + i) * DH:P + (TT + i + 1) * DH] for i in range(TT)]
        own_t = tab[:, P + 2 * TT * DH:P + 2 * TT * DH + 8]
        vis_t = [tab[:, NTAB - (TT - i) * 16:NTAB - (TT - i - 1) * 16] for i in range(TT)]
        hh = tmp[:, 0, 0:TT * CF].rearrange("p (t f) -> p t f", t=TT)
        w1_slot = [work[:, s * 2 * DM:(s + 1) * 2 * DM].rearrange("p (j n) -> p j n", n=CMP_HID) for s in range(2)]
        attn = work[:, 2 * DM:4 * DM].rearrange("p (t n) -> p t n", t=TT)
        z_t = [zwork[:, v * 512:(v + 1) * 512].rearrange("p (a t) -> p a t", a=2) for v in range(2)]
        zb = [zwork[:, DM + v * 512:DM + v * 512 + NJ * 2 * NCMP]
              .rearrange("p (j a n) -> p j a n", j=NJ, a=2) for v in range(2)]
        hid_row = [tmp[0:2 * NCMP, 0, v * CMP_HID:(v + 1) * CMP_HID] for v in range(2)]
        vbd = zwork[:, DM:DM + 512].rearrange("p (a d) -> p a d", d=DH)
        cmp_small = zwork[:, DM + 512:DM + 512 + 384]
        hid_k = cmp_small[:, 320:380].rearrange("p (e a n) -> p e a n", e=2, a=2)
        hid_v = cmp_small[:, 0:256].rearrange("p (e a n) -> p e a n", e=2, a=8)
        kbd = cmp_small[:, 256:320].rearrange("p (a b n) -> p a b n", a=2, b=2)
        probt = [zwork[:, s * 512:(s + 1) * 512] for s in range(2)]
        rope_a = silu[:, :, :].rearrange("p t f -> p (t f)")
        rope_b = sb("rope_b", [P, 512])
        gw = rope_b[:, 0:KT * GATES].rearrange("p (k n) -> p k n", k=KT)

        gate_t = zwork[0:GATES, DM + 512:DM + 512 + T]

        def prob_of(m, n):
            if m == "even" and n < 2:
                return probt[n]
            return work[:, n % 2 * DM:(n % 2 + 1) * DM]

        def mask(name):
            a, b = MASKS[name]
            return masks[:, a:b]

        free = [0]

        def stat(n):
            a = free[0]
            free[0] += n
            assert free[0] <= 320
            return stats[:, a:a + n]

        ss2 = [stat(TT) for _ in range(7)]
        rstd2 = [stat(TT) for _ in range(7)]
        ss = [[v[:, t:t + 1] for t in range(TT)] for v in ss2]
        rstd = [[v[:, t:t + 1] for t in range(TT)] for v in rstd2]
        newton, newton_2 = stat(1), stat(1)
        gate = [stat(GATES) for _ in range(TT)]

        first_landed = [sem("first_landed0"), sem("first_landed1")]
        raw_landed = [sem(f"raw_landed{i}") for i in range(RAW)]
        hi_done, lo_done = sem("hi_done"), sem("lo_done")
        down_used = sem("down_used")
        x_landed = [sem(f"x_landed{t}") for t in range(TT)]
        tab_landed, mask_landed, small_landed = sem("tab_landed"), sem("mask_landed"), sem("small_landed")
        gain_landed, w1_landed = sem("gain_landed"), [sem("w1_landed0"), sem("w1_landed1")]
        masks_ready, zeros_ready = sem("masks_ready"), sem("zeros_ready")
        gwh_ready, gwl_ready = sem("gwh_ready"), sem("gwl_ready")
        h_done, gained, ss_done, rstd_done = sem("h_done"), sem("gained"), sem("ss_done"), sem("rstd_done")
        xt_done, xh_done, xl_done = sem("xt_done"), sem("xh_done"), sem("xl_done")
        gu_done, silu_done, hh_done = sem("gu_done"), sem("silu_done"), sem("hh_done")
        ht_done, hth_done, htl_done, y_done = sem("ht_done"), sem("hth_done"), sem("htl_done"), sem("y_done")
        own, pool_own = sem("vector_own"), sem("pool_own")
        rope_ready = {m: sem(f"{m}_rope_ready") for m in ("even", "odd")}
        out_ready, out_landed = [sem("out_ready0"), sem("out_ready1")], sem("out_landed")
        mix = {}
        for m in ("even", "odd"):
            for n in ("proj_done", "proj_used", "rows_ready", "rows_t", "rows_copied", "scores_done",
                      "max_done", "prob_done", "pt_done", "first_copied", "second_copied", "pv_done",
                      "norm_done"):
                mix[m, n] = sem(f"{m}_{n}")
        gate_left, gate_copied, gate_turned = sem("gate_left"), sem("gate_copied"), sem("gate_turned")
        gate_done, gate_exp = sem("gate_done"), sem("gate_exp")
        zb_ready, hid_done, hid_ready = sem("zb_ready"), sem("hid_done"), sem("hid_ready")
        cmp_done, cmp_ready, cmp_masked = sem("cmp_done"), sem("cmp_ready"), sem("cmp_masked")
        hid_turned, hid_copied = sem("hid_turned"), sem("hid_copied")
        nsa_rows = sem("nsa_rows")
        sink_arg, sink_exp = sem("sink_arg"), sem("sink_exp")

        heads_q = qkv[:, 0:2 * DM].rearrange("p (a t) -> p a t", t=T)
        e_qu = qkv[:, 2 * DM:3 * DM].rearrange("p (a t) -> p a t", t=T)
        e_k = qkv[:, 3 * DM:3 * DM + 6 * T].rearrange("p (a t) -> p a t", t=T)
        e_v = qkv[:, 3 * DM + 6 * T:3 * DM + 6 * T + TT * 384].rearrange("p (t n) -> p t n", t=TT)
        o_k = qkv[:, 2 * DM:4 * DM].rearrange("p (a t) -> p a t", t=T)
        o_v = qkv[:, 4 * DM:6 * DM].rearrange("p (t n) -> p t n", t=TT)

        def make_units(m):
            units, groups = [], []
            if m == "even":
                for kind, tt in (("window", 0), ("window", 1), ("select", 0), ("select", 1),
                                 ("cmp", 0), ("wide", 0), ("cmp", 1), ("wide", 1)):
                    groups.append((kind, tt, 0 if kind == "window" else 512, stat(8), stat(8), stat(8)))
                    for kv in range(1 if kind == "cmp" else 2):
                        units.append((kind, tt, kv, len(groups) - 1, kind == "cmp" or kv == 1))
            else:
                for tt in range(TT):
                    groups.append(("odd", tt, 0, stat(8), stat(8), stat(8)))
                    for s in range(4):
                        units.append(("dilated", tt, s, len(groups) - 1, False))
                    units.append(("moba", tt, 0, len(groups) - 1, True))
            return units, groups

        UNITS_OF, GROUPS_OF = {}, {}
        for m in ("even", "odd"):
            UNITS_OF[m], GROUPS_OF[m] = make_units(m)

        def unit_halves(u):
            kind, tt, i, _, _ = u
            blocks = []
            if kind == "cmp":
                blocks = [(0, 0, 0, 0, True, True)]
            elif kind == "dilated":
                n = tt + 1
                for gr in range(3):
                    for kt in range(n):
                        blocks.append(((gr * n + kt) * P, kt, (gr * 4 + i) * DH, i * DH,
                                       gr == 0 and kt == 0, gr == 2 and kt == n - 1))
            else:
                for hd in range(4):
                    for kt in range(tt + 1):
                        vcol = {"window": 0, "select": 128, "wide": 256}.get(kind, 0) + i * DH
                        ocol = (4 * i + hd) * DH
                        if kind == "moba":
                            vcol, ocol = (12 + hd) * DH, (4 + hd) * DH
                        blocks.append((hd * (tt + 1) * P + kt * P, kt, vcol, ocol, kt == 0, kt == tt))
            return [blocks[a:a + 4] for a in range(0, len(blocks), 4)]

        HALF0 = {}
        for m in ("even", "odd"):
            n, HALF0[m] = 0, []
            for u in UNITS_OF[m]:
                HALF0[m].append(n)
                n += len(unit_halves(u))
            HALF0[m].append(n)

        COPIED = {}
        for m in ("even", "odd"):
            COPIED[m] = []
            for n, u in enumerate(UNITS_OF[m]):
                COPIED[m].append((mix[m, "first_copied"], n + 1))
                if len(unit_halves(u)) == 2:
                    COPIED[m].append((mix[m, "second_copied"], len(COPIED[m]) - n))

        LAST_HALF = {m: HALF0[m][-2] for m in ("even", "odd")}

        BATCHES = {
            "even": [[(0, 4, "q", 0)], [(0, 4, "k", 0), (512, 4, "k2", 4)], [(0, 2, "v", 0)],
                     [(0, 4, "q", 4), (512, 4, "qu", 0)]],
            "odd": [[(0, 4, "q", 0)], [(0, 4, "q", 4)], [(0, 4, "ko", 0)], [(0, 4, "ko", 4)], [], []],
        }

        def batch_index(m, b, tt):
            return sum(TT * len(x) for x in BATCHES[m][:b]) + (tt * len(BATCHES[m][b]) if tt else 0)

        block = ctx.enter_context(nc.Block())


        NB = {"even": E_BLOCKS, "odd": O_BLOCKS}
        U_M = {"even": U_E, "odd": U_O}
        B_M = {"even": B_E, "odd": B_O}
        D_M = {"even": D_E, "odd": D_O}
        XS_M = {"even": XS_E, "odd": XS_O}
        HALVES = {"even": 2, "odd": 1}
        U_OUT = {"even": U_E + 2 * E_BLOCKS, "odd": U_O + 2 * O_BLOCKS}
        NORM_M = {"even": 1, "odd": 4}
        NORM_F = [0, 2, 3, 5]
        U_TAIL = [U_F[f] + 3 * NCH - 1 - (0 if f < 3 else 2) for f in range(4)]

        def down_piece(w, place, p):
            if place is None:
                ring = down_hi if w is wide_hi else down_lo
                return ring[:, p, :]
            slot, half = place
            return w[:, slot, half * UNIT + p * DOWN:half * UNIT + (p + 1) * DOWN]

        TAIL = [((B_F[f] + NCH - 1) % 2, 0) for f in range(4)]
        SPLIT_AFTER = {"even": (3, 5, 7), "odd": (5, 6)}
        OUT_AT = {m: [None, ((B_M[m] + NB[m] - 1) % 2, 0), ((B_M[m] + NB[m] - 1) % 2, 1), None]
                  for m in ("even", "odd")}

        @block.sync
        def _(sp):
            sp.dma_start(h[:, 0, :], x[0:P, :]).then_inc(x_landed[0], 16)
            sp.dma_start(tab[:, :], consts[:, 0:NTAB]).then_inc(tab_landed, 16)
            for s in range(2):
                sp.dma_start(raw[:, s, 0:DOWN], stream[s, :, 0:DOWN]).then_inc(first_landed[s], 16)
                sp.dma_start(raw[:, s, DOWN:UNIT], stream[s, :, DOWN:UNIT]).then_inc(raw_landed[s], 16)
            sp.dma_start(h[:, 1, :], x[P:2 * P, :]).then_inc(x_landed[1], 16)
            sp.dma_start(raw[:, 2, :], stream[2, :, :]).then_inc(raw_landed[2], 16)
            with sp.Fori(1, UNITS // RAW) as j:
                for s in range(RAW):
                    sp.wait_ge(lo_done, j * (2 * RAW) + 2 * (s - RAW + 1))
                    sp.dma_start(raw[:, s, :], stream[j * RAW + s, :, :]).then_inc(raw_landed[s], 16)
            for n in range(UNITS // RAW * RAW, UNITS):
                sp.wait_ge(lo_done, 2 * (n - RAW + 1))
                sp.dma_start(raw[:, n % RAW, :], stream[n, :, :]).then_inc(raw_landed[n % RAW], 16)
            for tt in range(TT):
                for q in range(2):
                    w = slice(q * 512, (q + 1) * 512)
                    sp.wait_ge(out_ready[q], tt + 1)
                    sp.dma_start(out[tt * P:(tt + 1) * P, w], tmp[:, tt, w]).then_inc(out_landed, 16)
            sp.wait_ge(out_landed, 16 * 2 * TT)

        @block.gpsimd
        def _(pool):
            count = [0]

            def link(ins):
                count[0] += 1
                ins.then_inc(pool_own, 1)
                pool.wait_ge(pool_own, count[0])

            tt_op, ts_op = nc.gpsimd.tensor_tensor, nc.gpsimd.tensor_scalar

            def inverse_rms(i, tokens=(0, 1)):
                for tt in tokens:
                    r, v, a = rstd[i][tt], ss[i][tt], newton
                    pool.wait_ge(ss_done, TT * i + tt + 1)
                    link(ts_op(v, v, 1.0 / DM, EPS, ALU.mult, ALU.add))
                    link(ts_op(r.bitcast(I32), v.bitcast(I32), -0.5, float(0x5F3759DF), ALU.mult, ALU.add))
                    for step in range(3):
                        link(ts_op(a, r, r, v, ALU.mult, ALU.mult))
                        link(ts_op(a, a, -0.5, 1.5, ALU.mult, ALU.add))
                        if step < 2:
                            link(tt_op(r, r, a, ALU.mult))
                    tt_op(r, r, a, ALU.mult).then_inc(rstd_done, 1)

            def load_gain(i):
                pool.wait_ge(gained, 4 * i)
                pool.dma_start(gain[:, :], gains[i, :].partition_broadcast(P)).then_inc(gain_landed, 16)

            def rope_sums(m, b, tt, n):
                pool.wait_ge(rope_ready[m], n)
                a, c = (v.rearrange("p (a d) -> p a d", d=DH) for v in (rope_a, rope_b))
                rows = tmp[:, tt, :]
                if m == "even" and b == 1:
                    r4 = rows[:, 0:768].rearrange("p (a e d) -> p a e d", a=6, e=2)
                    link(tt_op(r4[:, :, 0, :], a[:, 0:6, :], c[:, 0:6, :], ALU.add))
                    last = tt_op(r4[:, :, 1, :], a[:, 0:6, :], c[:, 0:6, :], ALU.add)
                else:
                    last = tt_op(rows[:, 0:512].rearrange("p (a d) -> p a d", d=DH), a, c, ALU.add)
                last.then_inc(mix[m, "rows_ready"], len(BATCHES[m][b]))

            pool.dma_start(gain[:, :], gains[0, :].partition_broadcast(P)).then_inc(gain_landed, 16)
            pool.memset(zeros_b[:, :], 0.0).then_inc(zeros_ready, 1)
            inverse_rms(0)
            pool.wait_ge(raw_landed[2], 16)
            pool.dma_start(work[:, 0:NMASK], consts[:, NTAB:NTAB + NMASK]).then_inc(mask_landed, 16)
            pool.dma_start(gw, gate_w).then_inc(small_landed, 16)
            pool.dma_start(sink_b[:, :], sinks.partition_broadcast(P)).then_inc(small_landed, 16)
            pool.dma_start(pe_t[:, :, :], pe).then_inc(small_landed, 16)
            for d in range(2):
                pool.dma_start(w2k[:, :, d, :], w2[0]).then_inc(small_landed, 16)
            pool.dma_start(w2v[:, :, :], w2[1]).then_inc(small_landed, 16)
            pool.wait_ge(masks_ready, 2)
            for s in range(2):
                pool.dma_start(w1_slot[s], w1[s]).then_inc(w1_landed[s], 16)
            load_gain(1)
            for i in range(1, 7):
                inverse_rms(i, (0, 1) if i < 6 else (0,))
                if i < 6:
                    load_gain(i + 1)
                if i in (1, 4):
                    m, n = ("even", 0) if i == 1 else ("odd", 0)
                    nb = NB[m]
                    for b in range(nb):
                        for tt in range(TT):
                            if BATCHES[m][b] and not (m == "even" and b == 2):
                                n += 1
                                rope_sums(m, b, tt, n)
                        if m == "even" and b == nb - 1:
                            for s in range(2):
                                pool.wait_ge(hid_done, s + 1)
                                pool.dma_start(w1_slot[s], w1[2 + s]).then_inc(w1_landed[s], 16)

        @block.tensor
        def _(te):
            def mm(o, a, b, start=False, stop=False, **kw):
                return nc.tensor.matmul(o, a, b, start=start, stop=stop, **kw)

            def turn(o, a):
                return nc.tensor.transpose(o, a, ident)

            def wide_product(dst, tt, slot, first=None, halfway=None, split=None, fine=False):
                for k in range(KT):
                    if split is not None and k % (2 if fine else 4) == 0:
                        te.wait_ge(lo_done, split - ((3 - k // 2) if fine else (2 if k == 0 else 0)))
                    if k == KT // 2 and halfway is not None:
                        halfway()
                    if first is not None and k % 4 == 0:
                        te.wait_ge(xl_done, first + 2 * tt + k // 4 + 1)
                    xh, xl = xt_hi[:, k, tt * P:(tt + 1) * P], xt_lo[:, k, tt * P:(tt + 1) * P]
                    wh, wl = (w[:, slot, k * WIDE:(k + 1) * WIDE] for w in (wide_hi, wide_lo))
                    mm(dst, xh, wh, start=k == 0)
                    mm(dst, xh, wl)
                    last = mm(dst, xl, wh, stop=k == KT - 1)
                return last

            def down_part(tt, n, a_hi, a_lo, place, p, start=False, stop=False):
                c = slice(n * 512, (n + 1) * 512)
                w_hi, w_lo = down_piece(wide_hi, place, p)[:, c], down_piece(wide_lo, place, p)[:, c]
                mm(y[:, 2 * tt + n, :], a_hi, w_hi, start=start)
                mm(y[:, 2 * tt + n, :], a_hi, w_lo)
                return mm(y[:, 2 * tt + n, :], a_lo, w_hi, stop=stop)

            def finish(part, i, between=None):
                for tt, n in ((0, 0), (0, 1), (1, 0), (1, 1)):
                    part(tt, n).then_inc(y_done, 1)
                    if i < 6 and tt == 1:
                        norm_rows(i, 0, n)
                    if tt == 0 and n == 1 and between is not None:
                        between()

            def turn_rows(src, tt, q, first_bank=0):
                bank = (g, tp)[tt][(q + first_bank) % 2]
                for k in range(4):
                    c = (4 * q + k) * P
                    last = turn(bank[:, k * P:(k + 1) * P], src[:, tt, c:c + P])
                last.then_inc(xt_done, 1)

            def norm_rows(i, tt, q):
                if i == 0 and tt == 0 and q == 0:
                    te.wait_ge(tab_landed, 16)
                te.wait_ge(gained, 4 * i + 2 * tt + q + 1)
                turn_rows(tmp, tt, q)

            def norm_rows_1(i):
                for q in range(2):
                    norm_rows(i, 1, q)

            def ffn(f):
                i = NORM_F[f]

                def gate_up(c, tt, slot):
                    te.wait_ge(hh_done, c * 2 + (2 * NCH * f + tt - 1))
                    wide_product(g[tt][:, :], tt, slot,
                                 split=c * 6 + 2 * (U_F[f] - 1) if tt == 0 else None).then_inc(gu_done, 1)

                def turn_products(c):
                    te.wait_ge(hh_done, c * 2 + (2 * NCH * f + 2))
                    for ft in range(2):
                        for tt in range(TT):
                            last = turn(tp[ft][:, tt * P:(tt + 1) * P],
                                        hh[:, tt, ft * P:(ft + 1) * P])
                    last.then_inc(ht_done, 1)

                def down(tt, n, ft, place=None, stop=False):
                    w = slice(tt * P, (tt + 1) * P)
                    return down_part(tt, n, ht_hi[:, ft, w], ht_lo[:, ft, w], place, ft, stop=stop)

                for tt in range(TT):
                    wide_product(g[tt][:, :], tt, B_F[f] % 2, XS_N[i],
                                 split=2 * (I0_F[f] + 2) if tt == 0 else None, fine=f == 0,
                                 halfway=(lambda: norm_rows_1(i)) if tt == 0 and f else None).then_inc(gu_done, 1)
                    if tt == 0 and f == 0:
                        norm_rows_1(i)
                te.wait_ge(ss_done, TT * (i + 1))
                for n in range(4):
                    last = mm(y[:, n, :], zeros_b[:, 0:P], zeros_b[:, :], start=True)
                    if f == 0 and n >= 2:
                        last.then_inc(down_used, 1)
                turn_products(0)
                with te.Fori(0, (NCH - 1) // 2) as j:
                    for v in range(2):
                        c, before = j * 2 + (1 + v), j * 2 + v
                        slot = (B_F[f] + 1 + v) % 2
                        gate_up(c, 0, slot)
                        gate_up(c, 1, slot)
                        for ft in range(2):
                            te.wait_ge(htl_done, before * 2 + (2 * NCH * f + ft + 1))
                            te.wait_ge(lo_done, before * 6 + (2 * (U_F[f] + 2) + ft + 1))
                            for tt in range(TT):
                                for n in range(2):
                                    last = down(tt, n, ft)
                            last.then_inc(down_used, 1)
                            if ft == 0:
                                te.wait_ge(htl_done, before * 2 + (2 * NCH * f + 2))
                                turn_products(c)
                te.wait_ge(lo_done, 2 * (U_TAIL[f] + 1))

                te.wait_ge(htl_done, 2 * NCH * (f + 1) - 1)
                for n in range(2):
                    down(0, n, 0, TAIL[f])
                te.wait_ge(htl_done, 2 * NCH * (f + 1))

                def part(tt, n):
                    if tt:
                        down(tt, n, 0, TAIL[f])
                    return down(tt, n, 1, TAIL[f], stop=True)
                finish(part, i + 1)

            def mixer(m):
                s = {n: x for (a, n), x in mix.items() if a == m}
                i = NORM_M[m]
                units, groups = UNITS_OF[m], GROUPS_OF[m]

                def turn_batches(b, tt):
                    for a, (col, count, _, _) in enumerate(BATCHES[m][b]):
                        n = batch_index(m, b, tt) + a
                        te.wait_ge(s["rows_ready"], n + 1)
                        if n >= 2:
                            te.wait_ge(s["rows_copied"], n - 1)
                        for k in range(count):
                            last = turn(tp[n % 2][:, k * P:(k + 1) * P],
                                        tmp[:, tt, col + k * P:col + (k + 1) * P])
                        last.then_inc(s["rows_t"], 1)

                def gates(kh):
                    if kh == 0:
                        te.wait_ge(ss_done, TT * (i + 1))
                        te.wait_ge(gwl_ready, 1)
                    o = y[0:GATES, 0, 0:T]
                    for k in range(4 * kh, 4 * kh + 4):
                        mm(o, gw_hi[:, k, :], xt_hi[:, k, :], start=k == 0)
                        mm(o, gw_hi[:, k, :], xt_lo[:, k, :])
                        last = mm(o, gw_lo[:, k, :], xt_hi[:, k, :], stop=k == KT - 1)
                    if kh:
                        last.then_inc(gate_done, 1)

                def turn_gates():
                    te.wait_ge(gate_copied, 1)
                    for tt in range(TT):
                        last = nc.tensor.transpose(y[:, 1, tt * 32:tt * 32 + GATES], gate_t[:, tt * P:(tt + 1) * P],
                                                   ident[0:GATES, 0:GATES])
                    last.then_inc(gate_turned, 1)

                def compress(v):
                    hid = (y[:, 2, :], tp[1])[v][0:2 * NCMP, 0:CMP_HID]
                    te.wait_ge(zb_ready, 2 * (v + 1))
                    for jh in range(2):
                        te.wait_ge(w1_landed[jh], 16 * (v + 1))
                        for j in range(NJ // 2):
                            last = mm(hid, zb[v][:, jh * NJ // 2 + j, :, :],
                                      w1_slot[jh][:, j, :], start=jh == 0 and j == 0,
                                      stop=jh == 1 and j == NJ // 2 - 1)
                        last.then_inc(hid_done, 1)

                def scores(n):
                    kind, tt, a, _, _ = units[n]
                    bank, nk = y[:, 2 * (n % 2):2 * (n % 2) + 2, :], (tt + 1) * P
                    toks = slice(tt * P, (tt + 1) * P)
                    if kind == "dilated":
                        flat = bank.rearrange("p b n -> p (b n)")
                        dil = mask(f"dil{tt}")
                        off = (a % 2) * DH
                        for c in range(0, 3 * nk, 512):
                            w = min(512, 3 * nk - c)
                            mm(flat[:, c:c + w], ident_b[:, :], dil[:, c:c + w], start=True)
                            for gr in range(3):
                                if c <= gr * nk < c + w:
                                    pair = (4 * gr + a) // 2
                                    last = mm(flat[:, gr * nk:(gr + 1) * nk], heads_q[off:off + DH, pair, toks],
                                              o_k[off:off + DH, pair, 0:nk], stop=(gr + 1) * nk == c + w)
                    elif kind == "cmp":
                        v = bank[:, 0, 0:P].rearrange("p (a n) -> p a n", a=8)
                        mm(v, ident_b[:, :], mask(f"cmp{tt}").unsqueeze(1).broadcast_to([P, 8, 16]), start=True)
                        for pair in range(4):
                            last = mm(v[:, 2 * pair:2 * pair + 2, :], e_qu[:, pair, toks], kbd[:, pair // 2, :, :],
                                      stop=pair == 3)
                    else:
                        mk = mask(f"causal{tt}" if tt == 0 or kind != "window" else "band1")
                        pair0 = {"window": 2 * a, "select": 4 + 2 * a, "wide": 4 + 2 * a, "moba": 6}[kind]
                        for b in range(2):
                            v = bank[:, b, :].rearrange("p (a n) -> p a n", a=2)
                            for pos in range(2):
                                if kind == "moba":
                                    k = o_k[b * DH:(b + 1) * DH, 6 + pos, 0:nk]
                                else:
                                    k = e_k[b * DH:(b + 1) * DH,
                                            {"window": 0, "select": 2, "wide": 4}[kind] + a, 0:nk]
                                mm(v[:, pos, 0:nk], heads_q[b * DH:(b + 1) * DH, pair0 + pos, toks], k,
                                   start=pos == 0)
                            c0 = 0 if kind == "window" else tt * P
                            last = mm(v[:, :, c0:nk], ident_b[:, :],
                                      mk[:, c0:nk].unsqueeze(1).broadcast_to([P, 2, nk - c0]), stop=True)
                    last.then_inc(s["scores_done"], 1)

                def turn_probs(n):
                    kind = units[n][0]
                    if kind == "cmp":
                        te.wait_ge(cmp_masked, units[n][1] + 1)
                    else:
                        te.wait_ge(s["prob_done"], n + 1)
                    for a, blocks in enumerate(unit_halves(units[n])):
                        hf = HALF0[m][n] + a
                        if hf >= 2:
                            te.wait_ge(*COPIED[m][hf - 2])
                        for k, bl in enumerate(blocks):
                            last = turn(g[hf % 2][:, k * P:(k + 1) * P], prob_of(m, n)[:, bl[0]:bl[0] + P])
                        last.then_inc(s["pt_done"], 1)

                def values(n):
                    kind, tt, a, grp, _ = units[n]
                    if (n == 0 or units[n - 1][3] != grp) and grp >= 2:
                        te.wait_ge(s["norm_done"], grp - 1)
                    for a, blocks in enumerate(unit_halves(units[n])):
                        hf = HALF0[m][n] + a
                        te.wait_ge(*COPIED[m][hf])
                        if n == len(units) - 1 and a < HALVES[m]:
                            te.wait_ge(s["norm_done"], 1)
                            if m == "even":
                                te.wait_ge(nsa_rows, 1)
                            turn_rows(attn, 0, a, LAST_HALF[m])
                        for k, (_, kt, vcol, ocol, first, final) in enumerate(blocks):
                            o, v = tp[grp % 2][:, ocol:ocol + DH], (e_v if m == "even" else o_v)
                            if kind == "cmp":
                                o, v = tp[grp % 2][:, :], vbd
                            else:
                                v = v[:, kt, vcol:vcol + DH]
                            last = mm(o, probt[hf % 2][:, k * P:(k + 1) * P], v, start=first, stop=final)
                        last.then_inc(s["pv_done"], 1)

                def second_layer():
                    te.wait_ge(small_landed, 16 * 6)
                    te.wait_ge(hid_copied, 1)
                    for half in range(2):
                        mm(tp[1][:, P:P + 2 * NCMP], w2k[:, half, :, :], hid_k[:, half, :, :],
                           start=half == 0, stop=half == 1)
                    for half in range(2):
                        last = mm(tp[1][:, 2 * P:2 * P + DH], hid_v[:, half, :, :], w2v[:, half, :],
                                  start=half == 0, stop=half == 1)
                    last.then_inc(cmp_done, 1)

                def hidden_turned():
                    te.wait_ge(hid_ready, 2)
                    for v in range(2):
                        for half in range(2):
                            c = CMP_HID + (2 * v + half) * 32
                            last = nc.tensor.transpose(tp[1][:, c:c + 2 * NCMP],
                                                       hid_row[v][:, half * P:(half + 1) * P],
                                                       ident[0:2 * NCMP, 0:2 * NCMP])
                    last.then_inc(hid_turned, 1)

                nb = NB[m]
                for b in range(nb):
                    for tt in range(TT):
                        if b:
                            te.wait_ge(s["proj_used"], 2 * (b - 1) + tt + 1)
                        halfway = None
                        if b == 0 and tt == 0:
                            halfway = lambda: norm_rows_1(i)
                        elif m == "even" and b == 2 and tt == 0:
                            halfway = lambda: gates(0)
                        wide_product(g[tt][:, :], tt, (B_M[m] + b) % 2, XS_N[i] if b == 0 else None,
                                     split=None if tt else 2 * (U_M[m] + 2 * b - (0 if b else 1)),
                                     halfway=halfway).then_inc(s["proj_done"], 1)
                        if b:
                            turn_batches(b - 1, tt)
                        if m == "even" and b == 2 and tt == 0:
                            gates(1)
                        if m == "even" and b == nb - 1 and tt == 0:
                            turn_gates()
                        if m == "odd" and b == nb - 1 and tt == 0:
                            te.wait_ge(ss_done, TT * (i + 1))
                            te.wait_ge(s["rows_copied"], batch_index(m, nb, 0))
                            scores(0)
                            scores(1)
                if m == "even":
                    turn_batches(nb - 1, 0)
                    compress(0)
                    turn_batches(nb - 1, 1)
                    te.wait_ge(gate_left, TT)
                    te.wait_ge(s["rows_copied"], batch_index(m, nb - 1, 0))
                    scores(0)
                    te.wait_ge(hid_ready, 1)
                    scores(1)
                    te.wait_ge(s["rows_copied"], batch_index(m, nb, 0))
                    compress(1)
                for n in range(len(units)):
                    if n < 2:
                        te.wait_ge(s["proj_used"], 2 * nb - 1 + n)
                    turn_probs(n)
                    if n + 2 < len(units):
                        scores(n + 2)
                    if m == "even" and n == 1:
                        second_layer()
                    if m == "even" and n == 2:
                        te.wait_ge(cmp_ready, 1)
                    values(n)
                    if m == "even" and n == 0:
                        hidden_turned()

                nh = HALVES[m]
                pieces = 4 * nh
                u0 = U_OUT[m]

                def out_part(k, tt, n):
                    if k % 4 == 0:
                        te.wait_ge(xl_done, XS_M[m] + nh * tt + k // 4 + 1)
                    w = slice(tt * P, (tt + 1) * P)
                    return down_part(tt, n, xt_hi[:, k, w], xt_lo[:, k, w], OUT_AT[m][k // 2], k % 2,
                                     start=k == 0, stop=k == pieces - 1)
                early = min(4, pieces - 2)

                def early_pieces(tt):
                    for k in range(early):
                        te.wait_ge(lo_done, 2 * u0 + k + 1)
                        for n in range(2):
                            last = out_part(k, tt, n)
                        if tt and k < 2:
                            last.then_inc(down_used, 1)
                        if tt == 0 and k == 1:
                            te.wait_ge(s["norm_done"], len(groups))
                            if m == "even":
                                te.wait_ge(nsa_rows, TT)
                            for q in range(nh):
                                turn_rows(attn, 1, q)

                early_pieces(0)
                if m == "even":
                    early_pieces(1)
                for k in range(early, pieces - 2):
                    te.wait_ge(lo_done, 2 * u0 + k + 1)
                    for tt in range(TT):
                        for n in range(2):
                            last = out_part(k, tt, n)
                te.wait_ge(lo_done, 2 * u0 + pieces)

                def part(tt, n):
                    for k in range(pieces - 2, pieces):
                        last = out_part(k, tt, n)
                    return last
                finish(part, i + 1, (lambda: early_pieces(1)) if m == "odd" else None)

            def keep_warm(n):
                for _ in range(n):
                    mm(tp[0][:, :], zeros_b[:, 0:P], zeros_b[:, :], start=True, stop=True)

            te.wait_ge(zeros_ready, 1)
            keep_warm(13)
            for q in range(2):
                norm_rows(0, 0, q)
            keep_warm(8)
            ffn(0)
            mixer("even")
            ffn(1)
            ffn(2)
            mixer("odd")
            ffn(3)

        @block.scalar
        def _(act):
            def copy(o, a, **kw):
                return nc.scalar.activation(o, a, ACT.Copy, **kw)

            def split_wide(c, u, part, blk):
                slot = u % RAW
                act.wait_ge(raw_landed[slot], c * 16 + 16 * (u // RAW + 1))
                copy(wide_hi[:, blk, part * UNIT:(part + 1) * UNIT], raw[:, slot, :]).then_inc(hi_done, 2)

            def split_down(c, u, used=None, place=None):
                slot = u % RAW
                act.wait_ge(raw_landed[slot], c * 16 + 16 * (u // RAW + 1))
                for p in range(2):
                    if used is not None:
                        act.wait_ge(down_used, c * 2 + (used + p))
                    copy(down_piece(wide_hi, place, p), raw[:, slot, p * DOWN:(p + 1) * DOWN]).then_inc(hi_done, 1)

            def split_rows(n, tt, q, first_bank=0):
                act.wait_ge(xt_done, n + 1)
                copy(xt_hi[:, 4 * q:4 * q + 4, tt * P:(tt + 1) * P],
                     (g, tp)[tt][(q + first_bank) % 2][:, :].rearrange("p (k t) -> p k t", k=4)).then_inc(xh_done, 1)

            def norm_rows(i):
                def square(tt):
                    nc.scalar.activation(y[:, 2 * tt:2 * tt + 2, :], h[:, tt, :].rearrange("p (a n) -> p a n", a=2),
                                         ACT.Square, accum_out=ss[i][tt]).then_inc(ss_done, 1)
                if i == 0:
                    for n in range(2):
                        for p in range(2):
                            if n == 0:
                                split_rows(p, 0, p)
                            act.wait_ge((first_landed, raw_landed)[p][n], 16)
                            w = slice(p * DOWN, (p + 1) * DOWN)
                            copy(wide_hi[:, 0, n * UNIT + p * DOWN:n * UNIT + (p + 1) * DOWN],
                                 raw[:, n, w]).then_inc(hi_done, 1)
                    for tt in range(TT):
                        act.wait_ge(x_landed[tt], 16)
                        square(tt)
                    for q in range(2):
                        split_rows(2 + q, 1, q)
                    for n in range(2):
                        split_wide(0, U_F[0] + n, n, 1)
                    return
                for tt in range(TT):
                    if i < 6:
                        for q in range(2):
                            split_rows(XS_N[i] + 2 * tt + q, tt, q)
                    act.wait_ge(h_done, 4 * (i - 1) + 2 * tt + 2)
                    square(tt)

            def ffn(f):
                i = NORM_F[f]

                def silus(c, tt):
                    act.wait_ge(gu_done, c * 2 + (2 * NCH * f + tt + 1))
                    nc.scalar.activation(silu[:, tt, :], g[tt][:, 0:CF], ACT.Silu,
                                         scale=rstd[i][tt]).then_inc(silu_done, 1)

                def split_products(c, first=False):
                    act.wait_ge(ht_done, c + (NCH * f + 1))
                    for ft in range(2):
                        if not first:
                            act.wait_ge(down_used, c * 2 + (D_F[f] + ft - 1))
                        copy(ht_hi[:, ft, :], tp[ft][:, 0:T]).then_inc(hth_done, 1)

                def chunk(c, par, more=True, tail=False):
                    split_down(c, U_F[f] - 1, D_F[f] - 3)
                    if more:
                        act.wait_ge(gu_done, c * 2 + 2 * NCH * f)
                        split_wide(c, U_F[f], 0, (B_F[f] + par + 1) % 2)
                    silus(c, 0)
                    if more:
                        split_wide(c, U_F[f] + 1, 1, (B_F[f] + par + 1) % 2)
                    silus(c, 1)
                    if tail:
                        split_down(0, U_TAIL[f], place=TAIL[f])
                    split_products(c)

                norm_rows(i)
                if f:
                    for p in range(2):
                        split_wide(0, U_F[f] + p, p, (B_F[f] + 1) % 2)
                for tt in range(TT):
                    act.wait_ge(rstd_done, TT * i + tt + 1)
                    silus(0, tt)
                split_products(0, first=True)
                pairs = (NCH - 1) // 2
                with act.Fori(0, pairs - 1) as j:
                    for v in range(2):
                        chunk(j * 2 + (1 + v), 1 + v)
                if f == 0:
                    act.wait_ge(small_landed, 16 * 6)
                    copy(gw_hi[:, :, :], gw).then_inc(gwh_ready, 1)
                chunk(NCH - 2, (NCH - 2) % 2)
                chunk(NCH - 1, (NCH - 1) % 2, more=f < 3, tail=True)

            def mixer(m):
                s = {n: x for (a, n), x in mix.items() if a == m}
                i, nb, units = NORM_M[m], NB[m], UNITS_OF[m]

                def copy_batches(b, tt):
                    toks = slice(tt * P, (tt + 1) * P)
                    for a, (_, count, kind, at) in enumerate(BATCHES[m][b]):
                        n = batch_index(m, b, tt) + a
                        act.wait_ge(s["rows_t"], n + 1)
                        bank = tp[n % 2][:, :].rearrange("p (k t) -> p k t", k=4)
                        if kind == "q":
                            last = copy(heads_q[:, at:at + 4, toks], bank)
                        elif kind == "qu":
                            last = copy(e_qu[:, :, toks], bank)
                        elif kind == "ko":
                            last = copy(o_k[:, at:at + 4, toks], bank)
                        elif kind == "k":
                            last = copy(e_k[:, 0:4, toks], bank)
                        else:
                            z, src = (z_t[0], bank[:, 2:4, :]) if kind == "k2" else (z_t[1], bank[:, 0:2, :])
                            if kind == "k2":
                                copy(e_k[:, 4:6, toks], bank[:, 0:2, :])
                            copy(z[0:DH, :, toks], src[0:DH, :, :])
                            lo = 1 if tt == 0 else 0
                            last = copy(z[DH:P, :, tt * P + lo - 1:(tt + 1) * P - 1], src[DH:P, :, lo:P])
                        last.then_inc(s["rows_copied"], 1)

                def gelu(v):
                    act.wait_ge(hid_done, 2 * v + 2)
                    nc.scalar.activation(hid_row[v], (y[:, 2, :], tp[1])[v][0:2 * NCMP, 0:CMP_HID],
                                         ACT.Gelu_apprx_tanh).then_inc(hid_ready, 1)

                def copy_probs(n):
                    halves = unit_halves(units[n])
                    if len(halves) == 2:
                        hf = HALF0[m][n] + 1
                        c = slice(0, len(halves[1]) * P)
                        act.wait_ge(s["pt_done"], hf + 1)
                        act.wait_ge(s["pv_done"], hf - 1)
                        copy(probt[hf % 2][:, c], g[hf % 2][:, c]).then_inc(s["second_copied"], 1)

                norm_rows(i)
                for b in range(nb):
                    if b:
                        act.wait_ge(s["proj_done"], 2 * b)
                    for p in range(TT):
                        split_wide(0, U_M[m] + 2 * b + p, p, (B_M[m] + b + 1) % 2)
                        if m == "even" and b == nb - 1 and p == 0:
                            act.wait_ge(gate_done, 1)
                            copy(gate_t, y[0:GATES, 0, 0:T]).then_inc(gate_copied, 1)
                        if b:
                            copy_batches(b - 1, p)
                for tt in range(TT):
                    copy_batches(nb - 1, tt)
                    if m == "even" and tt == 0:
                        gelu(0)
                for n, (kind, tt, a, grp, final) in enumerate(units):
                    nk = (tt + 1) * P
                    _, _, _, nmax, den, r = GROUPS_OF[m][grp]
                    act.wait_ge(s["max_done"], n + 1)
                    if n >= 2:
                        act.wait_ge(s["pt_done"], HALF0[m][n - 1])
                    bank = y[:, 2 * (n % 2):2 * (n % 2) + 2, :]
                    if kind == "dilated":
                        last = nc.scalar.activation(prob_of(m, n)[:, 0:3 * nk],
                                                    bank.rearrange("p b n -> p (b n)")[:, 0:3 * nk], ACT.Exp,
                                                    bias=nmax[:, a:a + 1], scale=SCALE, accum_out=den[:, a:a + 1])
                    elif kind == "cmp":
                        last = nc.scalar.activation(prob_of(m, n)[:, 0:P], prob_of(m, n)[:, 0:P], ACT.Exp, scale=SCALE)
                    else:
                        for hd in range(4):
                            c = 4 * a + hd + (4 if kind == "moba" else 0)
                            last = nc.scalar.activation(prob_of(m, n)[:, hd * nk:(hd + 1) * nk],
                                                        bank[:, hd % 2, (hd // 2) * T:(hd // 2) * T + nk], ACT.Exp,
                                                        bias=nmax[:, c:c + 1], scale=SCALE,
                                                        accum_out=den[:, c:c + 1])
                    last.then_inc(s["prob_done"], 1)
                    if kind == "window" and final:
                        act.wait_ge(sink_arg, tt + 1)
                        nc.scalar.activation(r, r, ACT.Exp).then_inc(sink_exp, 1)
                    if n:
                        copy_probs(n - 1)
                    if n in SPLIT_AFTER[m]:
                        b = SPLIT_AFTER[m].index(n)
                        if b == 1:
                            act.wait_ge(s["proj_done"], 2 * nb)
                        split_down(0, U_OUT[m] + b, place=OUT_AT[m][b])
                    if m == "even" and n == 1:
                        gelu(1)
                        for tt in range(TT):
                            act.wait_ge(gate_left, tt + 1)
                            nc.scalar.activation(gate[tt], gate[tt], ACT.Exp).then_inc(gate_exp, 1)
                copy_probs(len(units) - 1)
                for tt in range(TT):
                    for q in range(HALVES[m]):
                        split_rows(XS_M[m] + HALVES[m] * tt + q, tt, q, 0 if tt else LAST_HALF[m])
                if m == "even":
                    split_down(0, U_OUT[m] + 3, D_M[m] + 1)

            ffn(0)
            mixer("even")
            ffn(1)
            ffn(2)
            mixer("odd")
            ffn(3)
            norm_rows(6)
            for tt in range(TT):
                act.wait_ge(rstd_done, TT * 6 + tt + 1)
                act.wait_ge(gained, 4 * 6 + 2 * tt + 1)
                copy(tmp[:, tt, 0:512], tmp[:, tt, 0:512], scale=rstd[6][tt]).then_inc(out_ready[0], 1)

        @block.vector
        def _(dve):
            count = [0]

            def link(ins):
                count[0] += 1
                ins.then_inc(own, 1)

            def settle():
                dve.wait_ge(own, count[0])

            tt_op, ts_op, stt = nc.vector.tensor_tensor, nc.vector.tensor_scalar, nc.vector.scalar_tensor_tensor

            def split_wide(c, u, part, blk):
                dve.wait_ge(hi_done, c * 6 + 2 * (u + 1))
                w = slice(part * UNIT, (part + 1) * UNIT)
                tt_op(wide_lo[:, blk, w], raw[:, u % RAW, :], wide_hi[:, blk, w].bitcast(F32),
                      ALU.subtract).then_inc(lo_done, 2)

            def split_down(c, u, place=None):
                for p in range(2):
                    dve.wait_ge(hi_done, c * 6 + (2 * u + p + 1))
                    tt_op(down_piece(wide_lo, place, p), raw[:, u % RAW, p * DOWN:(p + 1) * DOWN],
                          down_piece(wide_hi, place, p).bitcast(F32), ALU.subtract).then_inc(lo_done, 1)

            def split_rows(n, tt, q, first_bank=0):
                dve.wait_ge(xh_done, n + 1)
                w = (slice(None), slice(4 * q, 4 * q + 4), slice(tt * P, (tt + 1) * P))
                tt_op(xt_lo[w], (g, tp)[tt][(q + first_bank) % 2][:, :].rearrange("p (k t) -> p k t", k=4),
                      xt_hi[w].bitcast(F32), ALU.subtract).then_inc(xl_done, 1)

            def residual(i, tt, q):
                w = slice(q * 512, (q + 1) * 512)
                if i:
                    dve.wait_ge(y_done, 4 * (i - 1) + 2 * tt + q + 1)
                    ins = stt(h[:, tt, w], y[:, 2 * tt + q, :], 1.0 if i in (2, 5) else 0.5, h[:, tt, w],
                              ALU.mult, ALU.add)
                    ins.then_inc(h_done, 1)
                elif q == 0:
                    dve.wait_ge(x_landed[tt], 16)
                if tt == 0 and q == 0:
                    dve.wait_ge(gain_landed, 16 * (i + 1))
                if i:
                    dve.wait_ge(h_done, 4 * (i - 1) + 2 * tt + q + 1)
                tt_op(tmp[:, tt, w], h[:, tt, w], gain[:, w], ALU.mult).then_inc(gained, 1)

            def norm_rows(i):
                residual(i, 0, 0)
                residual(i, 0, 1)
                split_rows(XS_N[i], 0, 0)
                if i:
                    residual(i, 1, 0)
                    split_rows(XS_N[i] + 1, 0, 1)
                else:
                    for n in range(2):
                        for p in range(2):
                            if n == 0 and p:
                                split_rows(1, 0, 1)
                            dve.wait_ge(hi_done, 2 * n + p + 1)
                            w = slice(n * UNIT + p * DOWN, n * UNIT + (p + 1) * DOWN)
                            tt_op(wide_lo[:, 0, w], raw[:, n, p * DOWN:(p + 1) * DOWN],
                                  wide_hi[:, 0, w].bitcast(F32), ALU.subtract).then_inc(lo_done, 1)
                    residual(0, 1, 0)
                residual(i, 1, 1)
                for q in range(2):
                    split_rows(XS_N[i] + 2 + q, 1, q)

            def ffn(f):
                i = NORM_F[f]

                def products(c, tt):
                    dve.wait_ge(silu_done, c * 2 + (2 * NCH * f + tt + 1))
                    stt(hh[:, tt, :], g[tt][:, CF:2 * CF], rstd[i][tt], silu[:, tt, :], ALU.mult,
                        ALU.mult).then_inc(hh_done, 1)

                def split_products(c):
                    for ft in range(2):
                        dve.wait_ge(hth_done, c * 2 + (2 * NCH * f + ft + 1))
                        tt_op(ht_lo[:, ft, :], tp[ft][:, 0:T],
                              ht_hi[:, ft, :].bitcast(F32), ALU.subtract).then_inc(htl_done, 1)

                def chunk(c, par, more=True, tail=False):
                    split_down(c, U_F[f] - 1)
                    if more:
                        split_wide(c, U_F[f], 0, (B_F[f] + par + 1) % 2)
                    products(c, 0)
                    if more:
                        split_wide(c, U_F[f] + 1, 1, (B_F[f] + par + 1) % 2)
                    products(c, 1)
                    if tail:
                        split_down(0, U_TAIL[f], TAIL[f])
                    split_products(c)

                norm_rows(i)
                for p in range(2):
                    split_wide(0, U_F[f] + p, p, (B_F[f] + 1) % 2)
                for tt in range(TT):
                    products(0, tt)
                split_products(0)
                if f == 0:
                    prepare()
                pairs = (NCH - 1) // 2
                with dve.Fori(0, pairs - 1) as j:
                    for v in range(2):
                        chunk(j * 2 + (1 + v), 1 + v)
                if f == 0:
                    dve.wait_ge(small_landed, 16 * 6)
                    link(ts_op(nsink[:, :], sink_b[:, :], -1.0, None, ALU.mult))
                    dve.wait_ge(gwh_ready, 1)
                    tt_op(gw_lo[:, :, :], gw, gw_hi[:, :, :].bitcast(F32), ALU.subtract).then_inc(gwl_ready, 1)
                chunk(NCH - 2, (NCH - 2) % 2)
                chunk(NCH - 1, (NCH - 1) % 2, more=f < 3, tail=True)

            def mixer(m):
                s = {n: x for (a, n), x in mix.items() if a == m}
                i, nb, units, groups = NORM_M[m], NB[m], UNITS_OF[m], GROUPS_OF[m]

                def rotate(tt, n):
                    v = g[tt][:, 0:n * DH].rearrange("p (a d) -> p a d", d=DH)
                    ra = rope_a[:, 0:n * DH].rearrange("p (a d) -> p a d", d=DH)
                    rb = rope_b[:, 0:n * DH].rearrange("p (a d) -> p a d", d=DH)
                    r, hd = rstd[i][tt], DH // 2
                    link(stt(ra, v, r, cos_t[tt].unsqueeze(1).broadcast_to([P, n, DH]), ALU.mult, ALU.mult))
                    link(stt(rb[:, :, 0:hd], v[:, :, hd:DH], r,
                             sin_t[tt][:, 0:hd].unsqueeze(1).broadcast_to([P, n, hd]), ALU.mult, ALU.mult))
                    return ra, rb, stt(rb[:, :, hd:DH], v[:, :, 0:hd], r,
                                       sin_t[tt][:, hd:DH].unsqueeze(1).broadcast_to([P, n, hd]), ALU.mult, ALU.mult)

                def leave(b, tt):
                    used = 2 * b + tt + 1
                    dve.wait_ge(s["proj_done"], used)
                    kinds = BATCHES[m][b]
                    before = batch_index(m, b - 1, tt) + len(BATCHES[m][b - 1]) if b else 0
                    if kinds and before:
                        dve.wait_ge(s["rows_t"], before)
                    rows, bank = tmp[:, tt, :], g[tt]
                    if kinds and batch_index(m, b, tt):
                        dve.wait_ge(s["rows_ready"], batch_index(m, b, tt))
                    if m == "odd" and b >= 4:
                        ts_op(o_v[:, tt, (b - 4) * 512:(b - 3) * 512], bank[:, :], rstd[i][tt], None,
                              ALU.mult).then_inc(s["proj_used"], 1)
                    elif m == "even" and b == 1:
                        _, _, last = rotate(tt, 6)
                        link(last)
                        v = bank[:, 6 * DH:8 * DH].rearrange("p (a d) -> p a d", d=DH)
                        for d in range(2):
                            last = ts_op(rows[:, 768:1024].rearrange("p (a e d) -> p a e d", a=2, e=2)[:, :, d, :],
                                         v, rstd[i][tt], None, ALU.mult)
                            if d == 0:
                                link(last)
                        last.then_inc(s["proj_used"], 1)
                        settle()
                        dve.wait_ge(s["proj_used"], used)
                        dve.sem_inc(rope_ready[m], 1)
                    elif m == "even" and b == 2:
                        link(ts_op(e_v[:, tt, :], bank[:, 0:384], rstd[i][tt], None, ALU.mult))
                        v = bank[:, 6 * DH:8 * DH].rearrange("p (a d) -> p a d", d=DH)
                        for d in range(2):
                            last = ts_op(rows[:, 0:256].rearrange("p (a e d) -> p a e d", a=2, e=2)[:, :, d, :],
                                         v, rstd[i][tt], None, ALU.mult)
                            if d == 0:
                                link(last)
                        last.then_inc(s["proj_used"], 1)
                        dve.wait_ge(s["proj_used"], used)
                        dve.sem_inc(s["rows_ready"], 1)
                    else:
                        if m == "even" and b == 3:
                            link(ts_op(rows[:, 512:1024], bank[:, :], rstd[i][tt], None, ALU.mult))
                        _, _, last = rotate(tt, 8)
                        last.then_inc(s["proj_used"], 1)
                        settle()
                        dve.wait_ge(s["proj_used"], used)
                        dve.sem_inc(rope_ready[m], 1)

                def windows(v):
                    dve.wait_ge(s["rows_copied"], batch_index(m, 2 + v, 0))
                    z = z_t[v][:, :, :]
                    for a in range(2):
                        sa = bass.AP(tensor=z.tensor, offset=z.offset + a * T,
                                     ap=[list(z.ap[0]), [2, NJ], [CMP_STRIDE, NCMP]])
                        last = tt_op(zb[v][:, :, a, :], sa,
                                     pe_t[:, v, :].unsqueeze(2).broadcast_to([P, NJ, NCMP]), ALU.add)
                        last.then_inc(zb_ready, 1)

                def maxima(n):
                    kind, tt, a, grp, final = units[n]
                    nk = (tt + 1) * P
                    _, _, _, nmax, den, r = groups[grp]
                    bank = y[:, 2 * (n % 2):2 * (n % 2) + 2, :]
                    dve.wait_ge(s["scores_done"], n + 1)
                    if kind == "dilated":
                        w = slice(a, a + 1)
                        link(nc.vector.reduce_max(nmax[:, w], bank.rearrange("p b n -> p (b n)")[:, 0:3 * nk], AX))
                    elif kind == "cmp":
                        v = bank[:, 0, 0:P].rearrange("p (a n) -> p a n", a=8)
                        link(nc.vector.reduce_max(nmax, v, AX))
                        settle()
                        dve.wait_ge(s["pt_done"], HALF0[m][n - 1])
                        tt_op(prob_of(m, n)[:, 0:P].rearrange("p (a n) -> p a n", a=8), v,
                              nmax.unsqueeze(2).broadcast_to([P, 8, 16]), ALU.subtract).then_inc(s["max_done"], 1)
                        return
                    else:
                        c = 4 * a + (4 if kind == "moba" else 0)
                        w = slice(c, c + 4)
                        v = bank.rearrange("p b (a n) -> p b a n", a=2)[:, :, :, 0:nk]
                        link(nc.vector.reduce_max(nmax[:, w].rearrange("p (a b) -> p b a", b=2), v, AX))
                    settle()
                    if kind == "window":
                        stt(nmax[:, w], nmax[:, w], -SCALE, nsink[:, w], ALU.mult, ALU.min).then_inc(s["max_done"], 1)
                        if final:
                            dve.wait_ge(s["max_done"], n + 1)
                            tt_op(r, sink_b[:, :], nmax, ALU.add).then_inc(sink_arg, 1)
                    else:
                        ts_op(nmax[:, w], nmax[:, w], -SCALE, None, ALU.mult).then_inc(s["max_done"], 1)

                def cmp_sum(n):
                    _, tt, _, grp, _ = units[n]
                    den = groups[grp][4]
                    dve.wait_ge(s["prob_done"], n + 1)
                    pv = prob_of(m, n)[:, 0:P].rearrange("p (a n) -> p a n", n=16)
                    link(tt_op(pv, pv, vis_t[tt].unsqueeze(1).broadcast_to([P, 8, 16]), ALU.mult))
                    settle()
                    link(nc.vector.reduce_sum(den, pv, AX))
                    settle()
                    stt(den, den, 0.0, den, ALU.is_le, ALU.add).then_inc(cmp_masked, 1)

                def copy_probs(n):
                    hf, blocks = HALF0[m][n], unit_halves(units[n])[0]
                    c = slice(0, len(blocks) * P)
                    dve.wait_ge(s["pt_done"], hf + 1)
                    if hf >= 2:
                        dve.wait_ge(s["pv_done"], hf - 1)
                    nc.vector.tensor_copy(probt[hf % 2][:, c], g[hf % 2][:, c]).then_inc(s["first_copied"], 1)

                def normalise(grp, hf):
                    kind, tt, col, nmax, den, r = groups[grp]
                    if kind == "window":
                        dve.wait_ge(sink_exp, tt + 1)
                        link(tt_op(den, den, r, ALU.add))
                        settle()
                    link(nc.vector.reciprocal(r, den))
                    settle()
                    if kind in ("select", "wide", "cmp"):
                        ch = {"cmp": 0, "select": 1, "wide": 2}[kind]
                        link(tt_op(r, r, gate[tt].rearrange("p (a c) -> p c a", c=3)[:, ch, :], ALU.mult))
                        settle()
                    dve.wait_ge(s["pv_done"], hf)
                    o = tp[grp % 2][:, :].rearrange("p (a d) -> p a d", d=DH)
                    rb = r.unsqueeze(2).broadcast_to([P, 8, DH])
                    rows = attn[:, tt, col:col + 512].rearrange("p (a d) -> p a d", d=DH)
                    if kind in ("wide", "cmp"):
                        part = rope_a.rearrange("p (a d) -> p a d", d=DH)
                        tt_op(part, o, rb, ALU.mult).then_inc(s["norm_done"], 1)
                        dve.wait_ge(s["norm_done"], grp + 1)
                        last = tt_op(rows, rows, part, ALU.add)
                        if kind == "wide":
                            last.then_inc(nsa_rows, 1)
                        else:
                            link(last)
                            settle()
                    else:
                        tt_op(rows, o, rb, ALU.mult).then_inc(s["norm_done"], 1)

                def hidden():
                    settle()
                    dve.wait_ge(hid_turned, 1)
                    ht = tp[1][:, CMP_HID:CMP_HID + P].rearrange("p (v e n) -> p v e n", v=2, e=2)[:, :, :, 0:2 * NCMP]
                    link(nc.vector.tensor_copy(hid_k.rearrange("p e a n -> p e (a n)"), ht[:, 0, :, :]))
                    for e in range(2):
                        for a in range(2):
                            link(nc.vector.tensor_copy(
                                hid_v[:, e, 4 * a:4 * a + 4, 0:NCMP],
                                ht[:, 1, e, a * NCMP:(a + 1) * NCMP].unsqueeze(1).broadcast_to([P, 4, NCMP])))
                    settle()
                    dve.sem_inc(hid_copied, 1)

                def compressed():
                    dve.wait_ge(cmp_done, 1)
                    kc = tp[1][:, P:P + 2 * NCMP].rearrange("p (a n) -> p a n", a=2)
                    link(nc.vector.tensor_copy(kbd[0:DH, :, 0, 0:NCMP], kc[0:DH, :, :]))
                    link(nc.vector.tensor_copy(kbd[DH:P, :, 1, 0:NCMP], kc[DH:P, :, :]))
                    link(tt_op(vbd, tp[1][:, 2 * P:2 * P + DH].unsqueeze(1).broadcast_to([P, 8, DH]),
                               own_t.unsqueeze(2).broadcast_to([P, 8, DH]), ALU.mult))
                    settle()
                    dve.sem_inc(cmp_ready, 1)

                norm_rows(i)
                for b in range(nb):
                    for p in range(TT):
                        split_wide(0, U_M[m] + 2 * b + p, p, (B_M[m] + b + 1) % 2)
                        if b == 0:
                            dve.wait_ge(rstd_done, TT * i + p + 1)
                        if m == "even" and b == nb - 1 and p == 0:
                            windows(0)
                        if m == "even" and b == nb - 1 and p == 1:
                            dve.wait_ge(gate_turned, 1)
                            for tt in range(TT):
                                ts_op(gate[tt], y[:, 1, tt * 32:tt * 32 + GATES], rstd[i][tt], -1.0, ALU.mult,
                                      ALU.mult).then_inc(gate_left, 1)
                        if m == "odd" and b == nb - 1 and p == 1:
                            maxima(0)
                            maxima(1)
                        leave(b, p)
                if m == "even":
                    windows(1)
                    maxima(0)
                    maxima(1)
                    dve.wait_ge(hid_done, 4)
                    link(nc.vector.memset(cmp_small, 0.0))
                for n, u in enumerate(units):
                    copy_probs(n)
                    if n + 1 < len(units) and units[n + 1][0] == "cmp":
                        cmp_sum(n + 1)
                    if n and units[n - 1][4]:
                        normalise(units[n - 1][3], HALF0[m][n])
                    if n in SPLIT_AFTER[m]:
                        b = SPLIT_AFTER[m].index(n)
                        split_down(0, U_OUT[m] + b, OUT_AT[m][b])
                    if m == "even" and n == 2:
                        for tt in range(TT):
                            dve.wait_ge(gate_exp, tt + 1)
                            link(ts_op(gate[tt], gate[tt], 1.0, None, ALU.add))
                            settle()
                            link(nc.vector.reciprocal(gate[tt], gate[tt]))
                    if n + 2 < len(units):
                        maxima(n + 2)
                    if m == "even" and n == 0:
                        hidden()
                    if m == "even" and n == 1:
                        compressed()
                for tt in range(TT):
                    if tt:
                        normalise(units[-1][3], HALF0[m][-1])
                    for q in range(HALVES[m]):
                        split_rows(XS_M[m] + HALVES[m] * tt + q, tt, q, 0 if tt else LAST_HALF[m])
                if m == "even":
                    split_down(0, U_OUT[m] + 3)

            def prepare():
                dve.wait_ge(mask_landed, 16)
                nc.vector.tensor_copy(masks[:, :], work[:, 0:NMASK]).then_inc(masks_ready, 1)
                nc.vector.tensor_copy(ident_b[:, :], ident).then_inc(masks_ready, 1)

            ffn(0)
            mixer("even")
            ffn(1)
            ffn(2)
            mixer("odd")
            ffn(3)
            for tt in range(TT):
                for q in range(2):
                    residual(6, tt, q)
            for tt in range(TT):
                if tt:
                    rr, v, a = rstd[6][1], ss[6][1], newton_2
                    dve.wait_ge(ss_done, TT * 7)

                    def step(ins):
                        link(ins)
                        settle()

                    step(ts_op(v, v, 1.0 / DM, EPS, ALU.mult, ALU.add))
                    step(ts_op(rr.bitcast(I32), v.bitcast(I32), -0.5, float(0x5F3759DF), ALU.mult, ALU.add))
                    for _ in range(3):
                        step(ts_op(a, rr, rr, v, ALU.mult, ALU.mult))
                        step(ts_op(a, a, -0.5, 1.5, ALU.mult, ALU.add))
                        step(tt_op(rr, rr, a, ALU.mult))
                    dve.wait_ge(rstd_done, TT * 6 + 1)
                    dve.sem_inc(rstd_done, 1)
                dve.wait_ge(rstd_done, TT * 6 + tt + 1)
                dve.wait_ge(gained, 4 * 6 + 2 * tt + 2)
                ts_op(tmp[:, tt, 512:DM], tmp[:, tt, 512:DM], rstd[6][tt], None, ALU.mult).then_inc(out_ready[1], 1)


def kernel(**inputs):
    from concourse import bacc
    from concourse.bass_utils import run_bass_kernel_spmd

    a = {k: np.asarray(v) for k, v in inputs.items()}

    def wide_ffn(wi):
        v = wi.reshape(KT, P, 2, NCH, CF).transpose(3, 1, 0, 2, 4)
        return [c.reshape(P, 2, UNIT).transpose(1, 0, 2) for c in v]

    def wide_in(w):
        v = w.reshape(KT, P, -1, WIDE).transpose(2, 1, 0, 3)
        return [c.reshape(P, 2, UNIT).transpose(1, 0, 2) for c in v]

    def down_blocks(w):
        return [c.transpose(1, 0, 2).reshape(1, P, UNIT) for c in w.reshape(-1, 2, P, DOWN)]

    ew = a["even_w_in"][0]
    cols = {}
    at = 0
    for name, n in (("aq", 512), ("ak", 128), ("av", 128), ("bq", 512), ("kc", 128), ("vc", 128),
                    ("ks", 128), ("vs", 128), ("kw", 128), ("vw", 128), ("bg", GATES)):
        cols[name] = ew[:, at:at + n]
        at += n
    order = ("aq", "ak", "ks", "kw", "kc", "av", "vs", "vw", "vc", "bq")
    even_in = wide_in(np.concatenate([cols[n] for n in order], axis=1))
    ow = a["odd_w_in"][0]
    o = [ow[:, 0:768], ow[:, 768:1536], ow[:, 1536:2304], ow[:, 2304:2560], ow[:, 2560:2816], ow[:, 2816:3072]]
    odd_in = wide_in(np.concatenate([o[0], o[3], o[1], o[4], o[2], o[5]], axis=1))
    even_out, odd_out = down_blocks(a["even_w_out"][0]), down_blocks(a["odd_w_out"][0])
    ffns = [(wide_ffn(a["ffn_wi"][layer, s]), down_blocks(a["ffn_wo"][layer, s])) for layer in range(2) for s in range(2)]

    units = [ffns[0][0][0]]

    def ffn_units(f, following):
        wide, down = ffns[f]
        wide = wide + following
        for c in range(NCH):
            if c:
                units.append(down[c - 1])
            if c + 1 < len(wide):
                units.append(wide[c + 1])
        units.append(down[-1])

    ffn_units(0, even_in[:1])
    units += even_in[1:] + [ffns[1][0][0]] + even_out
    ffn_units(1, ffns[2][0][:1])
    ffn_units(2, odd_in[:1])
    units += odd_in[1:] + [ffns[3][0][0]] + odd_out
    ffn_units(3, [])
    stream = np.concatenate(units)
    assert stream.shape == (UNITS, P, UNIT)

    gains = np.stack([a["ffn_norm_pre"][0], a["mix_norm"][0], a["ffn_norm_post"][0],
                      a["ffn_norm_pre"][1], a["mix_norm"][1], a["ffn_norm_post"][1], a["final_norm"]])
    w1 = a["nsa_cmp_w1"][0].reshape(2, 2, NJ // 2, P, CMP_HID).transpose(0, 1, 3, 2, 4).reshape(4, P, NJ // 2, CMP_HID)
    arrays = {
        "x": a["x"][0],
        "gains": gains,
        "stream": stream,
        "gate_w": cols["bg"].reshape(KT, P, GATES).transpose(1, 0, 2),
        "w1": w1,
        "w2": a["nsa_cmp_w2"][0].reshape(2, 2, P, DH).transpose(0, 2, 1, 3),
        "pe": a["nsa_cmp_pe"][0].reshape(2, NJ, P).transpose(2, 0, 1),
        "sinks": a["even_sinks"][0],
        "consts": constants(),
    }
    arrays = {k: np.ascontiguousarray(v) for k, v in arrays.items()}
    nc = bacc.Bacc("TRN2", target_bir_lowering=False, num_devices=1)
    aps = [nc.dram_tensor(n, v.shape, F32, kind="ExternalInput").ap() for n, v in arrays.items()]
    out = nc.dram_tensor("out", (T, DM), F32, kind="ExternalOutput").ap()
    trunk(nc, *aps, out)
    r = run_bass_kernel_spmd(nc, [arrays], core_ids=[0])
    return r.results[0]["out"].reshape(1, T, DM)
```
